# Optimizing a Trainium2 kernel written in Bass

```python
import jax, jax.numpy as jnp
from jax import lax
import numpy as np

D_MODEL = 2048
BATCH = 1
SEQ = 256
DEPTH = 1

MIX_WIDTH = D_MODEL
ATTN_WIDTH = MIX_WIDTH // 2
REC_WIDTH = MIX_WIDTH - ATTN_WIDTH
N_ATTN_HEADS = 8
V_HEAD_DIM = ATTN_WIDTH // N_ATTN_HEADS
QK_NOPE_DIM = 128
QK_ROPE_DIM = 64
QK_HEAD_DIM = QK_NOPE_DIM + QK_ROPE_DIM
Q_LORA_RANK = 512
KV_LORA_RANK = 256
ROPE_THETA = 10000.0
Q_BLOCK = 128
N_REC_HEADS = 8
REC_HEAD_DIM = REC_WIDTH // N_REC_HEADS
CONV_WIDTH = 4
LRU_C = 8.0
N_PEER_HEADS = 8
PEER_TOPK = 16
N_KEYS = 128
N_EXPERTS = N_KEYS * N_KEYS
PEER_QUERY_DIM = 256
PEER_HALF = PEER_QUERY_DIM // 2
TOKEN_CHUNK = 128
EPS = 1e-6
OFF_CQ = 0
OFF_CKV = OFF_CQ + Q_LORA_RANK
OFF_KR = OFF_CKV + KV_LORA_RANK
OFF_XR = OFF_KR + QK_ROPE_DIM
OFF_YG = OFF_XR + REC_WIDTH
IN_COLS = OFF_YG + REC_WIDTH


def rms_norm(t, g):
    tf = t.astype(jnp.float32)
    y = tf * lax.rsqrt(jnp.mean(tf * tf, axis=-1, keepdims=True) + EPS)
    return (y * g.astype(jnp.float32)).astype(t.dtype)

def rope_tables(positions):
    half = QK_ROPE_DIM // 2
    inv_freq = ROPE_THETA ** (-jnp.arange(half, dtype=jnp.float32) / half)
    ang = positions.astype(jnp.float32)[..., None] * inv_freq
    return jnp.cos(ang), jnp.sin(ang)

def apply_rope(t, cos, sin):
    tf = t.astype(jnp.float32)
    t1, t2 = jnp.split(tf, 2, axis=-1)
    out = jnp.concatenate([t1 * cos - t2 * sin, t1 * sin + t2 * cos], axis=-1)
    return out.astype(t.dtype)

def causal_block_attention(q, k, v):
    S = q.shape[2]
    scale = QK_HEAD_DIM ** -0.5
    diag = jnp.tril(jnp.ones((Q_BLOCK, Q_BLOCK), dtype=bool))
    outs = []
    for blk in range(S // Q_BLOCK):
        start = blk * Q_BLOCK
        end = start + Q_BLOCK
        s = jnp.einsum('bhqd,bhkd->bhqk', q[:, :, start:end], k[:, :, :end],
                       preferred_element_type=jnp.float32) * scale
        mask = jnp.concatenate([jnp.ones((Q_BLOCK, start), dtype=bool), diag], axis=1)
        p = jax.nn.softmax(jnp.where(mask, s, -jnp.inf), axis=-1).astype(v.dtype)
        outs.append(jnp.einsum('bhqk,bhkd->bhqd', p, v[:, :, :end]))
    return jnp.concatenate(outs, axis=2)

def mla_group(c_q, c_kv, k_rope, cos, sin, q_norm_g, w_uq, kv_norm_g, w_ukv, q_head_g, k_head_g):
    B, S, _ = c_q.shape
    q = (rms_norm(c_q, q_norm_g) @ w_uq).reshape(B, S, N_ATTN_HEADS, QK_HEAD_DIM)
    kv = (rms_norm(c_kv, kv_norm_g) @ w_ukv).reshape(B, S, N_ATTN_HEADS, QK_NOPE_DIM + V_HEAD_DIM)
    k_nope, v = kv[..., :QK_NOPE_DIM], kv[..., QK_NOPE_DIM:]
    k_r = jnp.broadcast_to(k_rope[:, :, None, :], (B, S, N_ATTN_HEADS, QK_ROPE_DIM))
    k = jnp.concatenate([k_nope, k_r], axis=-1)
    q = rms_norm(q, q_head_g)
    k = rms_norm(k, k_head_g)
    c, s = cos[:, :, None, :], sin[:, :, None, :]
    q = jnp.concatenate([q[..., :QK_NOPE_DIM], apply_rope(q[..., QK_NOPE_DIM:], c, s)], axis=-1)
    k = jnp.concatenate([k[..., :QK_NOPE_DIM], apply_rope(k[..., QK_NOPE_DIM:], c, s)], axis=-1)
    o = causal_block_attention(q.transpose(0, 2, 1, 3), k.transpose(0, 2, 1, 3), v.transpose(0, 2, 1, 3))
    return o.transpose(0, 2, 1, 3).reshape(B, S, ATTN_WIDTH)

def _lin_combine(e1, e2):
    a1, b1 = e1
    a2, b2 = e2
    return a1 * a2, a2 * b1 + b2

def rglru_group(x_rec, y_gate, conv_w, conv_b, w_rg, b_rg, w_ig, b_ig, lam):
    B, S, W = x_rec.shape
    xp = jnp.pad(x_rec, ((0, 0), (CONV_WIDTH - 1, 0), (0, 0)))
    xc = conv_b + sum(xp[:, j:j + S] * conv_w[j] for j in range(CONV_WIDTH))
    xh = xc.reshape(B, S, N_REC_HEADS, REC_HEAD_DIM)
    r = jax.nn.sigmoid((jnp.einsum('bshi,hij->bshj', xh, w_rg).reshape(B, S, W) + b_rg).astype(jnp.float32))
    i = jax.nn.sigmoid((jnp.einsum('bshi,hij->bshj', xh, w_ig).reshape(B, S, W) + b_ig).astype(jnp.float32))
    log_a = -LRU_C * r * jax.nn.softplus(-lam.astype(jnp.float32))
    a = jnp.exp(log_a)
    mult = jnp.sqrt(-jnp.expm1(2.0 * log_a))
    b = mult * i * xc.astype(jnp.float32)
    _, h = lax.associative_scan(_lin_combine, (a, b), axis=1)
    out = jax.nn.gelu(y_gate.astype(jnp.float32), approximate=False) * h
    return out.astype(x_rec.dtype)

def peer_ffn(xn, w_q, keys1, keys2, u_tab, v_tab):
    B, S, D = xn.shape
    xt = xn.reshape((B * S) // TOKEN_CHUNK, TOKEN_CHUNK, D)

    def chunk(xc):
        q = (xc @ w_q).reshape(TOKEN_CHUNK, N_PEER_HEADS, 2, PEER_HALF).astype(jnp.float32)
        s1 = jnp.einsum('chd,hnd->chn', q[:, :, 0], keys1.astype(jnp.float32))
        s2 = jnp.einsum('chd,hnd->chn', q[:, :, 1], keys2.astype(jnp.float32))
        v1, i1 = lax.top_k(s1, PEER_TOPK)
        v2, i2 = lax.top_k(s2, PEER_TOPK)
        cand = (v1[..., :, None] + v2[..., None, :]).reshape(TOKEN_CHUNK, N_PEER_HEADS, PEER_TOPK * PEER_TOPK)
        top, pos = lax.top_k(cand, PEER_TOPK)
        e = (jnp.take_along_axis(i1, pos // PEER_TOPK, axis=-1) * N_KEYS
             + jnp.take_along_axis(i2, pos % PEER_TOPK, axis=-1))
        g = jax.nn.softmax(top, axis=-1)
        ug = jnp.take(u_tab, e, axis=0)
        act = jax.nn.gelu(jnp.einsum('chkd,cd->chk', ug, xc).astype(jnp.float32), approximate=False)
        vg = jnp.take(v_tab, e, axis=0)
        return jnp.einsum('chk,chkd->cd', (g * act).astype(xc.dtype), vg)

    return lax.map(chunk, xt).reshape(B, S, D)

def first_inputs(seed: int = 0) -> dict:
    key = jax.random.key(seed)
    ks = jax.random.split(key, 32)
    L, D = DEPTH, D_MODEL
    f32 = jnp.float32

    def nrm(k, shape, scale):
        return jax.random.normal(k, shape, f32) * scale

    def gain(k, n):
        return 1.0 + 0.05 * jax.random.normal(k, (L, n), f32)

    x = jax.random.normal(ks[0], (BATCH, SEQ, D), f32)
    start = jax.random.randint(ks[1], (BATCH, 1), 0, 4096, dtype=jnp.int32)
    positions = start + jnp.arange(SEQ, dtype=jnp.int32)[None, :]
    ac = jax.random.uniform(ks[2], (L, REC_WIDTH), f32, 0.9, 0.999)
    a0 = ac ** (1.0 / LRU_C)
    lru_lambda = jnp.log(a0) - jnp.log1p(-a0)
    return {
        "x": x,
        "positions": positions,
        "mix_norm_g": gain(ks[3], D),
        "w_in": nrm(ks[4], (L, D, IN_COLS), D ** -0.5),
        "q_norm_g": gain(ks[5], Q_LORA_RANK),
        "w_uq": nrm(ks[6], (L, Q_LORA_RANK, N_ATTN_HEADS * QK_HEAD_DIM), Q_LORA_RANK ** -0.5),
        "kv_norm_g": gain(ks[7], KV_LORA_RANK),
        "w_ukv": nrm(ks[8], (L, KV_LORA_RANK, N_ATTN_HEADS * (QK_NOPE_DIM + V_HEAD_DIM)), KV_LORA_RANK ** -0.5),
        "q_head_norm_g": gain(ks[9], QK_HEAD_DIM),
        "k_head_norm_g": gain(ks[10], QK_HEAD_DIM),
        "conv_w": nrm(ks[11], (L, CONV_WIDTH, REC_WIDTH), CONV_WIDTH ** -0.5),
        "conv_b": nrm(ks[12], (L, REC_WIDTH), 0.01),
        "w_rgate": nrm(ks[13], (L, N_REC_HEADS, REC_HEAD_DIM, REC_HEAD_DIM), REC_HEAD_DIM ** -0.5),
        "b_rgate": nrm(ks[14], (L, REC_WIDTH), 0.1),
        "w_igate": nrm(ks[15], (L, N_REC_HEADS, REC_HEAD_DIM, REC_HEAD_DIM), REC_HEAD_DIM ** -0.5),
        "b_igate": nrm(ks[16], (L, REC_WIDTH), 0.1),
        "lru_lambda": lru_lambda,
        "attn_out_norm_g": gain(ks[17], ATTN_WIDTH),
        "rec_out_norm_g": gain(ks[18], REC_WIDTH),
        "w_out": nrm(ks[19], (L, MIX_WIDTH, D), MIX_WIDTH ** -0.5),
        "ffn_norm_g": gain(ks[20], D),
        "peer_w_q": nrm(ks[21], (L, D, N_PEER_HEADS * PEER_QUERY_DIM), D ** -0.5),
        "peer_keys_1": nrm(ks[22], (L, N_PEER_HEADS, N_KEYS, PEER_HALF), PEER_HALF ** -0.5),
        "peer_keys_2": nrm(ks[23], (L, N_PEER_HEADS, N_KEYS, PEER_HALF), PEER_HALF ** -0.5),
        "peer_u": nrm(ks[24], (L, N_EXPERTS, D), D ** -0.5),
        "peer_v": nrm(ks[25], (L, N_EXPERTS, D), (N_PEER_HEADS * PEER_TOPK) ** -0.5),
    }

def first_block(x, positions, mix_norm_g, w_in, q_norm_g, w_uq, kv_norm_g, w_ukv, q_head_norm_g,
              k_head_norm_g, conv_w, conv_b, w_rgate, b_rgate, w_igate, b_igate, lru_lambda,
              attn_out_norm_g, rec_out_norm_g, w_out, ffn_norm_g, peer_w_q, peer_keys_1,
              peer_keys_2, peer_u, peer_v):
    cos, sin = rope_tables(positions)
    for l in range(DEPTH):
        h = rms_norm(x, mix_norm_g[l])
        proj = h @ w_in[l]
        c_q = proj[..., OFF_CQ:OFF_CKV]
        c_kv = proj[..., OFF_CKV:OFF_KR]
        k_rope = proj[..., OFF_KR:OFF_XR]
        x_rec = proj[..., OFF_XR:OFF_YG]
        y_gate = proj[..., OFF_YG:IN_COLS]
        attn = mla_group(c_q, c_kv, k_rope, cos, sin, q_norm_g[l], w_uq[l], kv_norm_g[l], w_ukv[l],
                         q_head_norm_g[l], k_head_norm_g[l])
        rec = rglru_group(x_rec, y_gate, conv_w[l], conv_b[l], w_rgate[l], b_rgate[l], w_igate[l],
                          b_igate[l], lru_lambda[l])
        mixed = jnp.concatenate([rms_norm(attn, attn_out_norm_g[l]), rms_norm(rec, rec_out_norm_g[l])], axis=-1)
        x = x + mixed @ w_out[l]
        x = x + peer_ffn(rms_norm(x, ffn_norm_g[l]), peer_w_q[l], peer_keys_1[l], peer_keys_2[l],
                         peer_u[l], peer_v[l])
    return x


DEPTH_2 = 2

CTX_LEN = 256
GRID_W = 64

POOL_WINDOWS = (2, 4, 8, 16)
POOL_W = D_MODEL // 2
POOL_GROUP = POOL_W // len(POOL_WINDOWS)
CONV_W = D_MODEL // 2
CONV_K = 3
EVEN_IN = 2 * POOL_W + 4 * CONV_W

HG_DK = 128
HG_HEADS = D_MODEL // HG_DK
HG_DV = D_MODEL // HG_HEADS
HG_K = HG_HEADS * HG_DK
HG_V = HG_HEADS * HG_DV
ODD_IN = 3 * HG_K + 2 * HG_V
CHUNK = 64

N_EVEN = (DEPTH_2 + 1) // 2
N_ODD = DEPTH_2 // 2


def rms_norm_2(x, g):
    xf = x.astype(jnp.float32)
    y = xf * lax.rsqrt(jnp.mean(xf * xf, axis=-1, keepdims=True) + EPS)
    return (y * g.astype(jnp.float32)).astype(x.dtype)

def box_mean(x, w, axis):
    n = x.shape[axis]
    cs = jnp.cumsum(x.astype(jnp.float32), axis=axis)
    pad = [(0, 0)] * x.ndim
    pad[axis] = (1, 0)
    cs = jnp.pad(cs, pad)
    t = jnp.arange(n)
    lo = jnp.maximum(t - w // 2, 0)
    hi = jnp.minimum(t + w // 2 - 1, n - 1)
    s = jnp.take(cs, hi + 1, axis=axis) - jnp.take(cs, lo, axis=axis)
    cnt = (hi - lo + 1).astype(jnp.float32).reshape((n,) + (1,) * (x.ndim - axis - 1))
    return (s / cnt).astype(x.dtype)

def multiscale_pool(v, pool_w, pool_scale, on_grid):
    b, n, _ = v.shape
    outs = []
    for gi, w in enumerate(POOL_WINDOWS):
        vg = v[..., gi * POOL_GROUP:(gi + 1) * POOL_GROUP]
        if on_grid:
            rows = n // GRID_W
            m = box_mean(box_mean(vg.reshape(b, rows, GRID_W, POOL_GROUP), w, 1), w, 2)
            m = m.reshape(b, n, POOL_GROUP)
        else:
            m = box_mean(vg, w, 1)
        outs.append(m - vg)
    pooled = jnp.stack(outs, axis=2)
    mixed = jnp.einsum('bngi,gio->bngo', pooled, pool_w).reshape(b, n, POOL_W)
    return mixed * pool_scale

def depthwise_conv3(u, w, bias):
    n = u.shape[1]
    up = jnp.pad(u, ((0, 0), (1, 1), (0, 0)))
    return up[:, :n] * w[0] + up[:, 1:n + 1] * w[1] + up[:, 2:] * w[2] + bias

def pool_conv_mixer(h, w_in, pool_w, pool_scale, conv_w, conv_b, w_out, on_grid):
    idx = [int(i) for i in np.cumsum([POOL_W, POOL_W, CONV_W, CONV_W, CONV_W])]
    a_v, a_g, b_x, b_b, b_c, b_g = jnp.split(h @ w_in, idx, axis=-1)
    a_out = multiscale_pool(a_v, pool_w, pool_scale, on_grid) * jax.nn.silu(a_g)
    b_out = b_b * depthwise_conv3(b_c * b_x, conv_w, conv_b) * jax.nn.silu(b_g)
    return jnp.concatenate([a_out, b_out], axis=-1) @ w_out

def _heads(t, d):
    return t.reshape(t.shape[0], t.shape[1], HG_HEADS, d)

def _chunks(t):
    b, n, hh, d = t.shape
    return t.reshape(b, n // CHUNK, CHUNK, hh, d)

def _rev(t, reverse):
    return jnp.flip(t, axis=1) if reverse else t

def hgrn2_gates(z, lb):
    zf = z.astype(jnp.float32)
    f = lb + (1.0 - lb) * jax.nn.sigmoid(zf)
    k = (1.0 - lb) * jax.nn.sigmoid(-zf)
    return _heads(k, HG_DK), _heads(jnp.log(f), HG_DK)

def chunk_state_scan(kc, vc, bc, s0, keep_starts):
    b_last = bc[:, :, -1]
    k_dec = kc * jnp.exp(b_last[:, :, None] - bc)
    ds = jnp.einsum('bnchk,bnchv->bnhkv', k_dec, vc)
    decay = jnp.exp(b_last)

    def step(s, inp):
        d, dsn = inp
        return d[..., None] * s + dsn, (s if keep_starts else None)

    s_fin, starts = lax.scan(step, s0, (jnp.moveaxis(decay, 1, 0), jnp.moveaxis(ds, 1, 0)))
    return s_fin, starts

def hgrn2_chunk_scan(q, k, v, logf, s0):
    qc, kc, vc = _chunks(q), _chunks(k), _chunks(v)
    bc = jnp.cumsum(_chunks(logf), axis=2)
    s_fin, starts = chunk_state_scan(kc, vc, bc, s0, True)
    starts = jnp.moveaxis(starts, 0, 1)
    q_dec = qc * jnp.exp(bc)
    k_inv = kc * jnp.exp(-bc)
    inter = jnp.einsum('bnchk,bnhkv->bnchv', q_dec, starts)
    scores = jnp.einsum('bnchk,bnshk->bnhcs', q_dec, k_inv)
    mask = jnp.tril(jnp.ones((CHUNK, CHUNK), dtype=bool))
    scores = jnp.where(mask, scores, 0.0)
    intra = jnp.einsum('bnhcs,bnshv->bnchv', scores, vc)
    o = (inter + intra).reshape(q.shape[0], q.shape[1], HG_HEADS, HG_DV)
    return o, s_fin

def hgrn2_final_state(k, v, logf, s0):
    bc = jnp.cumsum(_chunks(logf), axis=2)
    s_fin, _ = chunk_state_scan(_chunks(k), _chunks(v), bc, s0, False)
    return s_fin

def hgrn2_readout(o, g, onorm_g, w_out):
    b, n = o.shape[:2]
    o = o * lax.rsqrt(jnp.mean(o * o, axis=-1, keepdims=True) + EPS)
    o = o.reshape(b, n, HG_V) * onorm_g.astype(jnp.float32) * jax.nn.silu(g.astype(jnp.float32))
    return o.astype(g.dtype) @ w_out

def hgrn2_mixer(h_lat, h_ctx, w_in, onorm_g, w_out, lb_fwd, lb_bwd, ctx_out):
    idx = [int(i) for i in np.cumsum([HG_K, HG_K, HG_V, HG_K])]
    zf_l, zb_l, i_l, q_l, g_l = jnp.split(h_lat @ w_in, idx, axis=-1)
    if ctx_out:
        zf_c, zb_c, i_c, q_c, g_c = jnp.split(h_ctx @ w_in, idx, axis=-1)
        q_c = _heads(q_c.astype(jnp.float32), HG_DK)
    else:
        zf_c, zb_c, i_c = jnp.split(h_ctx @ w_in[:, :idx[2]], idx[:2], axis=-1)
    q_l = _heads(q_l.astype(jnp.float32), HG_DK)
    v_l = _heads(i_l.astype(jnp.float32), HG_DV)
    v_c = _heads(i_c.astype(jnp.float32), HG_DV)
    s0 = jnp.zeros((h_lat.shape[0], HG_HEADS, HG_DK, HG_DV), jnp.float32)
    outs_l, outs_c = [], []
    for lb, z_l, z_c, reverse in ((lb_fwd, zf_l, zf_c, False), (lb_bwd, zb_l, zb_c, True)):
        k_l, lf_l = hgrn2_gates(z_l, lb)
        k_c, lf_c = hgrn2_gates(z_c, lb)
        if ctx_out:
            o_c, s_ctx = hgrn2_chunk_scan(_rev(q_c, reverse), _rev(k_c, reverse),
                                          _rev(v_c, reverse), _rev(lf_c, reverse), s0)
            outs_c.append(_rev(o_c, reverse))
        else:
            s_ctx = hgrn2_final_state(_rev(k_c, reverse), _rev(v_c, reverse),
                                      _rev(lf_c, reverse), s0)
        o_l, _ = hgrn2_chunk_scan(_rev(q_l, reverse), _rev(k_l, reverse),
                                  _rev(v_l, reverse), _rev(lf_l, reverse), s_ctx)
        outs_l.append(_rev(o_l, reverse))
    y_l = hgrn2_readout(outs_l[0] + outs_l[1], g_l, onorm_g, w_out)
    y_c = hgrn2_readout(outs_c[0] + outs_c[1], g_c, onorm_g, w_out) if ctx_out else None
    return y_l, y_c

def second_inputs(seed: int = 0) -> dict:
    key = jax.random.key(seed)
    ks = jax.random.split(key, 18)
    D = D_MODEL

    def nrm(k, shape, s):
        return jax.random.normal(k, shape, jnp.float32) * s

    return {
        "x": nrm(ks[0], (BATCH, SEQ, D), 1.0),
        "c": nrm(ks[1], (BATCH, D), 1.0),
        "ctx": nrm(ks[2], (BATCH, CTX_LEN, D), 1.0),
        "c_ctx": nrm(ks[3], (D,), 1.0),
        "ada_w": nrm(ks[4], (DEPTH_2, D, 3 * D), 0.5 * D ** -0.5),
        "ada_b": nrm(ks[5], (DEPTH_2, 3 * D), 0.01),
        "pre_g": 1.0 + nrm(ks[6], (DEPTH_2, D), 0.05),
        "post_g": 1.0 + nrm(ks[7], (DEPTH_2, D), 0.05),
        "ev_w_in": nrm(ks[8], (N_EVEN, D, EVEN_IN), D ** -0.5),
        "ev_pool_w": nrm(ks[9], (N_EVEN, len(POOL_WINDOWS), POOL_GROUP, POOL_GROUP), POOL_GROUP ** -0.5),
        "ev_pool_scale": 1.0 + nrm(ks[10], (N_EVEN, POOL_W), 0.1),
        "ev_conv_w": nrm(ks[11], (N_EVEN, CONV_K, CONV_W), CONV_K ** -0.5),
        "ev_conv_b": nrm(ks[12], (N_EVEN, CONV_W), 0.01),
        "ev_w_out": nrm(ks[13], (N_EVEN, POOL_W + CONV_W, D), (POOL_W + CONV_W) ** -0.5),
        "od_w_in": nrm(ks[14], (N_ODD, D, ODD_IN), D ** -0.5),
        "od_onorm_g": 1.0 + nrm(ks[15], (N_ODD, HG_V), 0.05),
        "od_w_out": nrm(ks[16], (N_ODD, HG_V, D), HG_V ** -0.5),
        "lb_logits": nrm(ks[17], (2, DEPTH_2 + 1, HG_K), 0.1),
    }

def second_block(x, c, ctx, c_ctx, ada_w, ada_b, pre_g, post_g, ev_w_in, ev_pool_w,
              ev_pool_scale, ev_conv_w, ev_conv_b, ev_w_out, od_w_in, od_onorm_g,
              od_w_out, lb_logits):
    lb_table = jnp.cumsum(jax.nn.softmax(lb_logits.astype(jnp.float32), axis=1), axis=1)
    s_lat = jax.nn.silu(c)
    s_ctx = jax.nn.silu(c_ctx)
    for layer in range(DEPTH_2):
        last = layer == DEPTH_2 - 1
        shift, scale, gate = jnp.split((s_lat @ ada_w[layer] + ada_b[layer])[:, None, :], 3, axis=-1)
        h = rms_norm_2(x, pre_g[layer]) * (1.0 + scale) + shift
        need_ctx = (layer % 2 == 1) or not last
        if need_ctx:
            shift_c, scale_c, gate_c = jnp.split(s_ctx @ ada_w[layer] + ada_b[layer], 3)
            hc = rms_norm_2(ctx, pre_g[layer]) * (1.0 + scale_c) + shift_c
        if layer % 2 == 0:
            e = layer // 2
            y = pool_conv_mixer(h, ev_w_in[e], ev_pool_w[e], ev_pool_scale[e], ev_conv_w[e],
                                ev_conv_b[e], ev_w_out[e], True)
            if not last:
                yc = pool_conv_mixer(hc, ev_w_in[e], ev_pool_w[e], ev_pool_scale[e], ev_conv_w[e],
                                     ev_conv_b[e], ev_w_out[e], False)
        else:
            o = layer // 2
            y, yc = hgrn2_mixer(h, hc, od_w_in[o], od_onorm_g[o], od_w_out[o],
                                lb_table[0, layer], lb_table[1, layer], not last)
        x = x + gate * rms_norm_2(y, post_g[layer])
        if not last:
            ctx = ctx + gate_c * rms_norm_2(yc, post_g[layer])
    return x


def setup_inputs(seed=0):
    out = dict(first_inputs(seed))
    for name, value in second_inputs(seed + 1).items():
        if name != "x":
            out[name + "_2"] = value
    return out


def reference(
    x, positions, mix_norm_g, w_in, q_norm_g, w_uq, kv_norm_g, w_ukv, q_head_norm_g,
    k_head_norm_g, conv_w, conv_b, w_rgate, b_rgate, w_igate, b_igate, lru_lambda,
    attn_out_norm_g, rec_out_norm_g, w_out, ffn_norm_g, peer_w_q, peer_keys_1, peer_keys_2,
    peer_u, peer_v, c_2, ctx_2, c_ctx_2, ada_w_2, ada_b_2, pre_g_2, post_g_2, ev_w_in_2,
    ev_pool_w_2, ev_pool_scale_2, ev_conv_w_2, ev_conv_b_2, ev_w_out_2, od_w_in_2, od_onorm_g_2,
    od_w_out_2, lb_logits_2,
):
    x = first_block(
        x, positions, mix_norm_g, w_in, q_norm_g, w_uq, kv_norm_g, w_ukv, q_head_norm_g,
        k_head_norm_g, conv_w, conv_b, w_rgate, b_rgate, w_igate, b_igate, lru_lambda,
        attn_out_norm_g, rec_out_norm_g, w_out, ffn_norm_g, peer_w_q, peer_keys_1, peer_keys_2,
        peer_u, peer_v,
    )
    return second_block(
        x, c_2, ctx_2, c_ctx_2, ada_w_2, ada_b_2, pre_g_2, post_g_2, ev_w_in_2, ev_pool_w_2,
        ev_pool_scale_2, ev_conv_w_2, ev_conv_b_2, ev_w_out_2, od_w_in_2, od_onorm_g_2,
        od_w_out_2, lb_logits_2,
    )


_drawn_inputs = setup_inputs


def setup_inputs(seed=0):
    import zlib

    import numpy as np

    out = dict(_drawn_inputs(seed))
    spreads = {}
    factors = {'b_rgate': 4.283,
     'ffn_norm_g': 6.446,
     'ctx_2': 3.838,
     'c_ctx_2': 4.805,
     'ada_b_2': 4.229,
     'post_g_2': 3.686,
     'ev_pool_scale_2': 4.089,
     'ev_conv_b_2': 25.399,
     'od_onorm_g_2': 5.823,
     'lb_logits_2': 3.789}
    for name, (base, spread) in spreads.items():
        noise = np.random.default_rng([zlib.crc32(name.encode()), seed]).standard_normal(out[name].shape)
        drawn = base * np.exp(spread * noise) if base else spread * noise
        out[name] = __import__('jax').numpy.asarray(drawn.astype(out[name].dtype))
    for name, factor in factors.items():
        out[name] = (out[name] * factor).astype(out[name].dtype)
    return out
```

```python
import math
from contextlib import ExitStack

import numpy as np
import concourse.bass as bass
import concourse.mybir as mybir

ALU = mybir.AluOpType
ACT = mybir.ActivationFunctionType
AX = mybir.AxisListType
F32 = mybir.dt.float32
F32R = mybir.dt.float32r
I32 = mybir.dt.int32
U32 = mybir.dt.uint32
BF16 = mybir.dt.bfloat16

P = 128
D = 2048
KT = D // P
S = 256
TT = S // P
EPS = 1e-6
COLS = 2048
RAW, HI = 4, 2

NH = 8
QKD, NOPE, ROPE, VD = 192, 128, 64, 128
QR, KVR = 512, 256
CQW = QR + KVR + ROPE
REC = 1024
RH = REC // P
KEYS = 128
TOPK = 16
PH = 8
TILES = 128
HALF = TILES // 2
WINDOWS = (2, 4, 8, 16)
GRID_W = 64
HG = 16
CH = 64

SEGMENTS = [
    ("in_tok", 8, "dve"), ("in_ch", 16, "dve"), ("ada_conv", 8, "raw"), ("gates", 1, "pool"),
    ("ada_lru", 16, "raw"), ("ada_cq", 4, "raw"), ("uq", 3, "pool"), ("ukv", 2, "pool"),
    ("ada_rope", 8, "raw"), ("out", 16, "dve"), ("wq", 16, "dve"), ("keys", 1, "dve"),
    ("ada_top", 28, "raw"),
    ("ada_g0", 8, "raw"), ("u0", HALF, "dve"), ("v0", HALF, "dve"),
    ("ada_g1", 8, "raw"), ("u1", HALF, "dve"), ("v1", HALF, "dve"),
    ("ev_a", 8, "pool"), ("pool", 1, "pool"), ("ev_b", 40, "pool"), ("ev_out", 16, "pool"),
    ("ada_post", 16, "raw"), ("od_v", 16, "pool"), ("od_heads", 64, "pool"), ("od_out", 16, "dve"),
]
BASE, KIND, RANK = {}, {}, {}
_n = 0
_done = {"pool": 0, "dve": 0, "raw": 0}
for _name, _count, _kind in SEGMENTS:
    BASE[_name], KIND[_name], RANK[_name] = _n, _kind, _done[_kind]
    _n += _count
    _done[_kind] += _count
CHUNKS = _n

PV_PARTS = [("mix_g", 16), ("q_g", 4), ("kv_g", 2), ("conv_w", 32), ("conv_b", 8), ("b_rg", 8),
            ("b_ig", 8), ("lam", 8), ("attn_g", 8), ("rec_g", 8), ("ffn_g", 16), ("pre_g", 32),
            ("ada_b", 64), ("pool_scale", 8), ("conv2_w", 24), ("conv2_b", 8), ("onorm", 16),
            ("lb", 96), ("c", 16), ("c_ctx", 16)]
PV = {}
_n = 0
for _name, _count in PV_PARTS:
    PV[_name] = (_n, _n + _count)
    _n += _count
PVN = _n
CN_PARTS = [("ident", P), ("ones", P), ("iota", P), ("iota16", 16), ("causal", P), ("inv_freq", 32),
            ("sel_lat", P), ("sel_ctx", P), ("sel2", 2)]
CN = {}
_n = 0
for _name, _count in CN_PARTS:
    CN[_name] = (_n, _n + _count)
    _n += _count
CNN = _n


COUNT = {name: count for name, count, _ in SEGMENTS}
RUNS = [["gates"], ["uq", "ukv"], ["ev_a", "pool", "ev_b", "ev_out"], ["od_v", "od_heads"]]
_columns = [(layer, n) for layer in range(2) for n in range(8)]
ADA = _columns[:12] + [(0, n) for n in range(8, 12)] + _columns[12:] + [(1, n) for n in range(8, 12)]
ADA_AT = [(name, c) for name, count, _ in SEGMENTS if name.startswith("ada_") for c in range(count)]

LRU_C = 8.0
ROUND = 1.5 * 2.0 ** 23
_two_pi = 2 * math.pi
_c1 = 6.28125
_c2 = float(np.float32(round((_two_pi - _c1) * 2 ** 21) / 2 ** 21))
TWO_PI = (_c1, _c2, _two_pi - _c1 - _c2)
PI_BELOW = 3.1415925


NORM_KINDS = ("ss", "ms", "sqrt", "diag", "turned", "full", "hi", "lo")
NORMS = [("n1", (2, 1, 1, 2, 16, 16, 4, 4)), ("recx", (0, 0, 0, 0, 0, 8, 2, 2)),
         ("cq", (4, 2, 1, 4, 6, 6, 3, 3)), ("ao", (2, 1, 1, 2, 8, 8, 2, 2)),
         ("n2", (2, 1, 1, 2, 16, 16, 4, 4)), ("q", (0, 0, 0, 0, 0, 16, 4, 4)),
         ("n3", (4, 1, 1, 4, 16, 16, 4, 4)), ("p0", (4, 1, 1, 0, 0, 0, 0, 0)),
         ("n4", (4, 1, 1, 4, 16, 16, 4, 4)), ("p1", (2, 1, 1, 0, 0, 0, 0, 0))]
NORM_BASE = {key: {kind: sum(c[k] for _, c in NORMS[:n]) for k, kind in enumerate(NORM_KINDS)}
             for n, (key, _) in enumerate(NORMS)}


class Own:

    def __init__(self, eng, label, sem):
        self.eng, self.label, self.sem = eng, label, sem
        self.count = {}

    def started(self, ins, tell=None):
        name = tell or self.label
        ins.then_inc(self.sem(name), 1)
        self.count[name] = self.count.get(name, 0) + 1
        return name

    def __call__(self, ins, tell=None):
        name = self.started(ins, tell)
        self.eng.wait_ge(self.sem(name), self.count[name])


def build(nc, d, out):
    ctx = ExitStack()
    with ctx:
        def sb(name, cols, dt=F32):
            return ctx.enter_context(nc.sbuf_tensor(name, [P, cols], dt))

        sems = {}

        def sem(name):
            if name not in sems:
                sems[name] = ctx.enter_context(nc.semaphore(name))
            return sems[name]

        def next_byte():
            return -(-nc.sbuf_base // 32) * 32

        def f32r_name(name, cols, at_byte):
            return nc.alloc_sbuf_tensor_at(name, [P, cols], F32R, offset=at_byte)

        raw_at = next_byte()
        raw = [sb(f"raw{i}", COLS) for i in range(RAW)]
        lo = [f32r_name(f"lo{i}", COLS, raw_at + 4 * i * COLS) for i in range(RAW)]
        hi = [sb(f"hi{i}", COLS, F32R) for i in range(HI)]
        params = sb("params_sb", PVN)
        consts = sb("consts_sb", CNN)
        small = sb("small", 768)
        diag_at = sb("diag", 4 * P)
        gqk_sb = sb("qk_gains", 2 * QKD)
        ARENA = 37888
        arena_at = next_byte()
        arena = sb("arena", ARENA)
        arena_f32r = {}
        ps = [ctx.enter_context(nc.psum_tensor(f"ps{i}", [P, 512], F32)) for i in range(8)]
        scratch = nc.dram_tensor("latent_spill", (P, TT * D), F32, kind="Internal").ap()

        def pv(name, k=0, n=None):
            a, b = PV[name]
            return params[:, a + k:(a + k + n if n else b)]

        def cn(name):
            a, b = CN[name]
            return consts[:, a:b]

        def at(off, n):
            assert off + n <= ARENA, (off, n)
            return arena[:, off:off + n]

        def at_r(off, n):
            assert off + n <= ARENA, (off, n)
            if (off, n) not in arena_f32r:
                arena_f32r[off, n] = f32r_name(f"arena_f32r_{off}_{n}", n, arena_at + 4 * off)
            return arena_f32r[off, n][:, :]

        RES_AT, X_AT = 0, TT * D
        res = at(RES_AT, TT * D).rearrange("p (t d) -> p t d", t=TT)

        def operand(n, kt=KT, off=X_AT):
            return [a.rearrange("p (k n) -> p k n", k=kt) for a in
                    (at_r(off, kt * n), at_r(off + kt * n, kt * n), at(off + kt * n, kt * n))]

        landed = [sem(f"landed{i}") for i in range(RAW)]
        used = sem("chunks_used")
        split = {"pool": sem("split_by_pool"), "dve": sem("split_by_dve")}
        hi_by_act = sem("hi_by_act")

        def wait_landed(eng, i, turn=None, step=0):
            v = 16 * (i // RAW + 1)
            eng.wait_ge(landed[i % RAW], v if turn is None else turn * (16 * step // RAW) + v)

        def take(pe, seg, c, turn=None, step=0):
            i = BASE[seg] + c
            if KIND[seg] == "raw":
                wait_landed(pe, i, turn, step)
                return raw[i % RAW], None
            v = RANK[seg] + c + 1
            pe.wait_ge(split[KIND[seg]], v if turn is None else turn * step + v)
            return hi[i % HI], lo[i % RAW]

        def wait_product(eng, seg, c, turn=None, step=0):
            v = BASE[seg] + c + 1
            eng.wait_ge(used, v if turn is None else turn * step + v)

        def norm_wait(eng, key, kind, n):
            eng.wait_ge(sem("norm_" + kind), NORM_BASE[key][kind] + n)

        def kind_of(i):
            return next(kind for name, count, kind in SEGMENTS if BASE[name] <= i < BASE[name] + count)

        def rank_of(i, only=None):
            n = 0
            for name, count, kind in SEGMENTS:
                if kind != "raw" and (only is None or kind == only):
                    n += max(0, min(i - BASE[name], count))
            return n

        def act_part(act, i, turn=None, step=0):
            if i >= CHUNKS or kind_of(i) == "raw":
                return
            wait_landed(act, i, turn, step)
            before = i - HI
            while turn is None and before >= 0 and kind_of(before) == "raw":
                before -= HI
            if before >= 0:
                act.wait_ge(used, before + 1 if turn is None else turn * step + before + 1)
            act.activation(hi[i % HI][:, :], raw[i % RAW][:, :], ACT.Copy).then_inc(hi_by_act, 1)

        def dve_part(dve, i, turn=None, step=0):
            if i >= CHUNKS or kind_of(i) != "dve":
                return
            v = rank_of(i) + 1
            dve.wait_ge(hi_by_act, v if turn is None else turn * step + v)
            dve.tensor_tensor(lo[i % RAW][:, :], raw[i % RAW][:, :], hi[i % HI][:, :].bitcast(F32),
                              ALU.subtract).then_inc(split["dve"], 1)

        meet = sem("stage_done")
        met = {}

        def rejoin(eng, key):
            met[key] = met.get(key, 0) + 1
            eng.drain().then_inc(meet, 1)
            eng.wait_ge(meet, 3 * met[key])

        def channel_product(pe, seg, c, dst, X, n, turn=None, step=0, kt=KT, off=0, last=True, first=0):
            whi, wlo = take(pe, seg, c, turn, step)
            wl = wlo[:, :]
            for k in range(kt):
                cs = slice(off + k * P, off + (k + 1) * P)
                for j, (w, x) in enumerate(((whi[:, cs], X[0]), (whi[:, cs], X[1]), (wl[:, cs], X[0]))):
                    mm = pe.matmul(dst, w, x[:, first + k, 0:n], start=k == 0 and j == 0,
                                   stop=k == kt - 1 and j == 2)
            if last:
                mm.then_inc(used, 1)
            return mm

        def token_product(pe, seg, c, banks, X, kts, width, k0, first, last):
            whi, wlo = take(pe, seg, c)
            wl = wlo[:, :]
            for k in range(kts):
                cs = slice(k * width, (k + 1) * width)
                for t, bank in banks:
                    ts = slice(t * P, (t + 1) * P)
                    for j, (w, x) in enumerate(((whi[:, cs], X[0]), (whi[:, cs], X[1]), (wl[:, cs], X[0]))):
                        mm = pe.matmul(bank, x[:, k0 + k, ts], w, start=first and k == 0 and j == 0,
                                       stop=last and k == kts - 1 and j == 2)
            mm.then_inc(used, 1)


        ident, ones = cn("ident"), cn("ones")

        _at = [0]

        def cols(n):
            _at[0] += n
            assert _at[0] <= 768
            return small[:, _at[0] - n:_at[0]]

        ss, rs = cols(8), cols(8)
        diag = diag_at[:, :].rearrange("p (t n) -> p t n", t=4)

        X = operand(S)
        cq = at(12288, TT * CQW).rearrange("p (t n) -> p t n", t=TT)
        XRW = S + 3
        xr = at(13952, RH * XRW).rearrange("p (h n) -> p h n", h=RH)
        yg = at(16032, RH * S)

        par_in = sem("params_in")
        x_in = sem("x_in")
        junk = at(ARENA - D, D)
        relu_lam, one_plus, lnw = cols(8), cols(8), cols(8)
        silu_c = cols(32)
        pos = cols(2)
        posi = cols(2).bitcast(I32)
        angle = cols(64)
        turn_, cosv, sinv = cols(64), cols(64), cols(64)
        sp = cols(16)
        lbc = cols(2 * HG)
        omlb = cols(2 * HG)
        gqk = gqk_sb[:, :]


        def act_setup(act, own):
            act.dma_start(params[:, :], d["params"]).then_inc(par_in, 16)
            act.dma_start(consts[:, :], d["consts"]).then_inc(par_in, 16)
            act.dma_start(posi, d["positions"]).then_inc(par_in, 16)
            act.dma_start(gqk[:, 0:192], d["q_head_g"].broadcast_to([P, 192])).then_inc(par_in, 16)
            act.dma_start(gqk[:, 192:384], d["k_head_g"].broadcast_to([P, 192])).then_inc(par_in, 16)
            for t in range(TT):
                act.dma_start(res[:, t, :], d["x"][t * P:(t + 1) * P, :]).then_inc(x_in, 16)
            act.wait_ge(par_in, 80)
            act.wait_ge(sem("negated_lam"), 1)
            own(act.activation(sp[:, 0:8], sp[:, 0:8], ACT.Exp, scale=-1.0), "exp_lam")
            act.wait_ge(sem("lb_shifted"), 1)
            own(act.activation(pv("lb"), pv("lb"), ACT.Exp), "lb_exp")
            act.wait_ge(sem("one_plus"), 1)
            own(act.activation(lnw, one_plus, ACT.Ln), "ln_lam")
            act.wait_ge(x_in, 16 * TT)

        def act_n1(act, own):
            def first_parts(act):
                for i in range(HI):
                    act_part(act, i)
            act_norm(act, own, "n1", [res[:, t, :] for t in range(TT)], S, between=first_parts)

        def act_angles(act, own):
            act.wait_ge(sem("angles"), 1)
            own(act.activation(sinv, angle, ACT.Sin))
            own(act.activation(cosv, turn_, ACT.Sin))
            own(act.activation(silu_c, params[:, PV["c"][0]:PV["c_ctx"][1]], ACT.Silu))

        def dve_n1(dve, own):
            dve_rms(dve, own, "n1", TT)
            dve_diag(dve, own, "n1", TT)
            for i in range(HI):
                dve_part(dve, i)
            dve_norm(dve, own, "n1", TT, S, lambda k, j: pv("mix_g", k, 1), None)

        def dve_setup(dve, own):
            own(dve.memset(xr[:, :, 0:3], 0.0))
            dve.wait_ge(par_in, 80)
            lam = pv("lam")
            own(dve.tensor_scalar(relu_lam, lam, -1.0, 0.0, ALU.mult, ALU.max))
            own(dve.scalar_tensor_tensor(sp[:, 0:8], lam, -1.0, lam, ALU.mult, ALU.max), "negated_lam")
            lb = pv("lb").rearrange("p (d l h) -> p d l h", d=2, l=3)
            l0, l1, l2 = lb[:, :, 0, :], lb[:, :, 1, :], lb[:, :, 2, :]
            lo = lbc.rearrange("p (d h) -> p d h", d=2)
            om = omlb.rearrange("p (d h) -> p d h", d=2)
            own(dve.tensor_tensor(lo, l0, l1, ALU.max))
            own(dve.tensor_tensor(lo, lo, l2, ALU.max))
            for k, part in enumerate((l0, l1, l2)):
                own(dve.tensor_tensor(part, part, lo, ALU.subtract), "lb_shifted" if k == 2 else None)
            dve.wait_ge(sem("exp_lam"), 1)
            own(dve.tensor_scalar(one_plus, sp[:, 0:8], 1.0, None, ALU.add), "one_plus")
            own(dve.tensor_scalar(sp[:, 8:16], one_plus, -1.0, None, ALU.add))
            own(dve.tensor_tensor(sp[:, 0:8], sp[:, 0:8], sp[:, 8:16], ALU.subtract))
            own(dve.reciprocal(sp[:, 8:16], one_plus))
            own(dve.tensor_tensor(sp[:, 0:8], sp[:, 0:8], sp[:, 8:16], ALU.mult))
            own(dve.tensor_tensor(sp[:, 0:8], sp[:, 0:8], relu_lam, ALU.add))
            dve.wait_ge(sem("ln_lam"), 1)
            own(dve.tensor_tensor(sp[:, 0:8], sp[:, 0:8], lnw, ALU.add))
            own(dve.tensor_scalar(sp[:, 8:16], sp[:, 0:8], -LRU_C, None, ALU.mult))
            own(dve.tensor_scalar(sp[:, 0:8], sp[:, 0:8], LRU_C, None, ALU.mult))
            dve.wait_ge(sem("lb_exp"), 1)
            own(dve.tensor_tensor(lo, l0, l1, ALU.add))
            own(dve.tensor_tensor(om, lo, l2, ALU.add))
            own(dve.reciprocal(om, om))
            own(dve.tensor_tensor(lo, lo, om, ALU.mult))
            own(dve.tensor_scalar(omlb, lbc, -1.0, 1.0, ALU.mult, ALU.add))

        def dve_angles(dve, own):
            own(dve.tensor_copy(pos, posi))
            for t in range(TT):
                own(dve.tensor_scalar(angle[:, t * 32:t * 32 + 32], cn("inv_freq"), pos[:, t:t + 1], None, ALU.mult))
            own(dve.tensor_scalar(turn_, angle, 1.0 / (2 * math.pi), ROUND, ALU.mult, ALU.add))
            own(dve.tensor_scalar(turn_, turn_, -ROUND, None, ALU.add))
            for part in TWO_PI:
                own(dve.scalar_tensor_tensor(angle, turn_, -part, angle, ALU.mult, ALU.add))
            own(dve.tensor_scalar(angle, angle, PI_BELOW, -PI_BELOW, ALU.min, ALU.max))
            own(dve.scalar_tensor_tensor(turn_, angle, -1.0, angle, ALU.mult, ALU.max))
            own(dve.tensor_scalar(turn_, turn_, -1.0, math.pi / 2, ALU.mult, ALU.add), "angles")

        def act_norm(act, own, key, tiles, n, width=D, cols_at=0, kts=KT, group=4, off=0, X=None,
                     between=None, arrived=None):
            X = X or operand(n)
            for t, tile in enumerate(tiles):
                if t == 2 and arrived:
                    arrived()
                own(act.activation(junk[:, 0:width], tile, ACT.Square, accum_out=ss[:, cols_at + t:cols_at + t + 1]),
                    "norm_ss")
            norm_wait(act, key, "ms", 1)
            own(act.activation(rs[:, cols_at:cols_at + len(tiles)], ss[:, cols_at:cols_at + len(tiles)], ACT.Sqrt), "norm_sqrt")
            if between:
                between(act)
            act_hi(act, key, X, n, kts, group, off)

        def act_hi(act, key, X, n, kts, group, off=0):
            for g in range(kts // group):
                norm_wait(act, key, "full", group * (g + 1))
                ks = slice(off + g * group, off + (g + 1) * group)
                act.activation(X[0][:, ks, 0:n], X[2][:, ks, 0:n], ACT.Copy).then_inc(sem("norm_hi"), 1)

        def dve_lo(dve, key, X, n, g, group, off=0):
            norm_wait(dve, key, "hi", g + 1)
            ks = slice(off + g * group, off + (g + 1) * group)
            dve.tensor_tensor(X[1][:, ks, 0:n], X[2][:, ks, 0:n], X[0][:, ks, 0:n].bitcast(F32),
                              ALU.subtract).then_inc(sem("norm_lo"), 1)

        def dve_rms(dve, own, key, T, width=D, cols_at=0):
            c = slice(cols_at, cols_at + T)
            norm_wait(dve, key, "ss", T)
            own(dve.tensor_scalar(ss[:, c], ss[:, c], 1.0 / width, EPS, ALU.mult, ALU.add), "norm_ms")
            norm_wait(dve, key, "sqrt", 1)
            own(dve.reciprocal(rs[:, c], rs[:, c]))

        def dve_diag(dve, own, key, T, cols_at=0):
            for t in range(T):
                own(dve.tensor_scalar(diag[:, t, :], ident, rs[:, cols_at + t:cols_at + t + 1], None, ALU.mult),
                    "norm_diag")

        def dve_norm(dve, own, key, T, n, scale, bias, kts=KT, group=4, off=0, X=None, span=None):
            X = X or operand(n)
            for k in range(kts):
                norm_wait(dve, key, "turned", k + 1)
                for lo_, hi_, j in (span or ((0, n, 0),)):
                    b = bias(k, j) if bias else 0.0
                    mm = dve.tensor_scalar(X[2][:, off + k, lo_:hi_], ps[k % 8][:, lo_:hi_], scale(k, j), b,
                                           ALU.mult, ALU.add)
                mm.then_inc(sem("norm_full"), 1)
                if k % group == group - 1 and k >= group:
                    dve_lo(dve, key, X, n, k // group - 1, group, off)
            dve_lo(dve, key, X, n, kts // group - 1, group, off)

        def pe_norm(pe, key, tiles, kts=KT):
            norm_wait(pe, key, "diag", len(tiles))
            for k in range(kts):
                if k >= 8:
                    norm_wait(pe, key, "full", k - 7)
                for t, tile in enumerate(tiles):
                    mm = pe.matmul(ps[k % 8][:, t * P:(t + 1) * P], tile(k), diag[:, t, :], start=True, stop=True)
                mm.then_inc(sem("norm_turned"), 1)

        res_tiles = [lambda k, t=t: res[:, t, k * P:(k + 1) * P] for t in range(TT)]

        def pe_in(pe):
            pe_norm(pe, "n1", res_tiles)
            norm_wait(pe, "n1", "full", KT)
            for c in range(8):
                norm_wait(pe, "n1", "lo", c // 2 + 1)
                w = take(pe, "in_tok", c)
                wl = w[1][:, :]
                half = CQW // 2
                for k in range(2):
                    for t in range(TT):
                        for j in range(2):
                            cs = slice(k * CQW + j * half, k * CQW + (j + 1) * half)
                            ts = slice(t * P, (t + 1) * P)
                            for q, (a, b) in enumerate(((X[0], w[0]), (X[1], w[0]), (X[0], wl))):
                                mm = pe.matmul(ps[2 * t + j][:, 0:half], a[:, 2 * c + k, ts], b[:, cs],
                                               start=c == 0 and k == 0 and q == 0, stop=c == 7 and k == 1 and q == 2)
                mm.then_inc(used, 1)
            for c in range(16):
                if c >= 4:
                    pe.wait_ge(sem("xr_kept" if c - 4 < 8 else "yg_kept"), (c - 4) % 8 + 1)
                channel_product(pe, "in_ch", c, ps[4 + c % 4][:, 0:S], X, S)

        def dve_in(dve, own):
            dve_n1(dve, own)
            dve_angles(dve, own)
            for c in range(8):
                dve_part(dve, BASE["in_tok"] + c + HI)
            wait_product(dve, "in_tok", 7)
            for t in range(TT):
                for j in range(2):
                    own(dve.tensor_copy(cq[:, t, j * (CQW // 2):(j + 1) * (CQW // 2)], ps[2 * t + j][:, 0:CQW // 2]))
            for c in range(16):
                dve_part(dve, BASE["in_ch"] + c + HI)
                if c < 8:
                    wait_product(dve, "in_ch", c)
                    dve.tensor_copy(xr[:, c, 3:3 + S], ps[4 + c % 4][:, 0:S]).then_inc(sem("xr_kept"), 1)

        def act_in(act, own):
            act_n1(act, own)
            for c in range(16):
                if c == 5:
                    act_angles(act, own)
                act_part(act, BASE["in_tok"] + c + HI)
            for c in range(8, 16):
                act_part(act, BASE["in_ch"] + c + HI)
                wait_product(act, "in_ch", c)
                act.activation(yg[:, (c - 8) * S:(c - 7) * S], ps[4 + c % 4][:, 0:S], ACT.Gelu).then_inc(sem("yg_kept"), 1)

        rows = at(36864, 1024).rearrange("p (b n) -> p b n", b=2)
        ada_cols = cols(128)
        sc2 = silu_c.rearrange("p (s k) -> p k s", s=2)

        def ada_product(pe, g, bank, chunks=range(4)):
            for c in chunks:
                w, _ = take(pe, *ADA_AT[4 * g + c])
                for k in range(4):
                    mm = pe.matmul(bank[0:2, :], sc2[:, 4 * c + k, :], w[:, k * 512:(k + 1) * 512],
                                   start=c == 0 and k == 0, stop=c == 3 and k == 3)
                mm.then_inc(used, 1)

        def ada_row(act, g, bank, rows=rows):
            wait_product(act, *ADA_AT[4 * g + 3])
            if g >= 2:
                act.wait_ge(sem("spread"), g - 1)
            act.activation(rows[0:2, g % 2, :], bank[0:2, :], ACT.Copy).then_inc(sem("row_kept"), 1)

        def ada_spread(pe, g, bank, rows=rows):
            pe.wait_ge(sem("row_kept"), g + 1)
            for j in range(4):
                mm = pe.matmul(bank[:, 2 * j:2 * j + 2], rows[0:2, g % 2, j * P:(j + 1) * P], cn("sel2")[0:2, :],
                               start=True, stop=True)
            mm.then_inc(sem("spread"), 1)

        def columns_kept(eng, g):
            eng.wait_ge(sem("cols_kept"), sum(n < 8 for _, n in ADA[:g]))

        def ada_columns(act, g, bank):
            layer, n = ADA[g]
            act.wait_ge(sem("spread"), g + 1)
            act.activation(ada_cols[:, 64 * layer + 8 * n:64 * layer + 8 * n + 8], bank[:, 0:8], ACT.Copy).then_inc(sem("cols_kept"), 1)

        XCo = operand(S, RH, X_AT)
        r_buf, i_buf = at(8192, RH * S), at(10240, RH * S)
        xcf, t1, t2 = at(18080, RH * S), at(20128, RH * S), at(22176, RH * S)
        eight = lambda b: b.rearrange("p (h n) -> p h n", h=RH)

        def dve_rec(dve, own):
            dve_cq_rms(dve, own)
            xc = eight(xcf)
            for h in range(RH):
                own(dve.tensor_scalar(xc[:, h, :], xr[:, h, 0:S], pv("conv_w", h, 1), pv("conv_b", h, 1), ALU.mult, ALU.add))
                for j in range(1, 4):
                    own(dve.scalar_tensor_tensor(xc[:, h, :], xr[:, h, j:j + S], pv("conv_w", 8 * j + h, 1),
                                                 xc[:, h, :], ALU.mult, ALU.add), "conv" if j == 3 else None)
            dve.wait_ge(sem("xc_hi"), 1)
            own(dve.tensor_tensor(XCo[1], eight(xcf), XCo[0].bitcast(F32), ALU.subtract), "xc_lo")
            dve.wait_ge(sem("tanh_a"), 1)
            own(dve.tensor_scalar(r_buf, t2, 1.0, None, ALU.add))
            own(dve.reciprocal(r_buf, r_buf))
            own(dve.scalar_tensor_tensor(t2, t2, 2.0, r_buf, ALU.mult, ALU.mult), "one_minus_a2")
            dve.wait_ge(sem("mult"), 1)
            own(dve.tensor_tensor(t2, t2, i_buf, ALU.mult))
            own(dve.tensor_tensor(t2, t2, xcf, ALU.mult))
            own(dve.memset(eight(t1)[:, :, 0:1], 0.0))
            own(dve.tensor_tensor_scan(r_buf, t1, t2, 0.0, ALU.mult, ALU.add))
            own(dve.tensor_tensor(r_buf, r_buf, yg, ALU.mult), "rec_out")
            dve.wait_ge(sem("rec_sum"), 1)
            rb = t2[:, 0:S]
            own(dve.tensor_scalar(rb, ps[0][:, 0:S], 1.0 / REC, EPS, ALU.mult, ALU.add), "rec_ms")
            dve.wait_ge(sem("rec_sqrt"), 1)
            own(dve.reciprocal(rb, rb))
            for h in range(RH):
                dve.scalar_tensor_tensor(X[2][:, 8 + h, :], eight(r_buf)[:, h, :], pv("rec_g", h, 1), rb,
                                         ALU.mult, ALU.mult).then_inc(sem("norm_full"), 1)
            for g in range(2):
                dve_lo(dve, "recx", X, S, g, 4, 8)

        def act_cq_rms(act, own):
            squares = at(29312, QR)
            for t in range(TT):
                own(act.activation(squares, cq[:, t, 0:QR], ACT.Square, accum_out=ss[:, 4 + t:5 + t]), "norm_ss")
                own(act.activation(squares[:, 0:KVR], cq[:, t, QR:QR + KVR], ACT.Square, accum_out=ss[:, 6 + t:7 + t]), "norm_ss")
            norm_wait(act, "cq", "ms", 2)
            own(act.activation(rs[:, 4:8], ss[:, 4:8], ACT.Sqrt), "norm_sqrt")

        def dve_cq_rms(dve, own):
            norm_wait(dve, "cq", "ss", 4)
            own(dve.tensor_scalar(ss[:, 4:6], ss[:, 4:6], 1.0 / QR, EPS, ALU.mult, ALU.add), "norm_ms")
            own(dve.tensor_scalar(ss[:, 6:8], ss[:, 6:8], 1.0 / KVR, EPS, ALU.mult, ALU.add), "norm_ms")
            norm_wait(dve, "cq", "sqrt", 1)
            own(dve.reciprocal(rs[:, 4:8], rs[:, 4:8]))
            dve_diag(dve, own, "cq", 4, 4)

        def act_rec(act, own):
            act_cq_rms(act, own)
            ada_row(act, 0, ps[0])
            act_part(act, BASE["gates"])
            act.wait_ge(sem("conv"), RH)
            own(act.activation(XCo[0], eight(xcf), ACT.Copy), "xc_hi")
            ada_row(act, 1, ps[1])
            for g in range(2):
                ada_columns(act, g, ps[g])
            wait_product(act, "gates", 0)
            for h in range(RH):
                own(act.activation(eight(r_buf)[:, h, :], ps[h][:, 0:S], ACT.Sigmoid, bias=pv("b_rg", h, 1)))
                own(act.activation(eight(i_buf)[:, h, :], ps[h][:, S:2 * S], ACT.Sigmoid, bias=pv("b_ig", h, 1)), "gates_read")
            for h in range(RH):
                own(act.activation(eight(t1)[:, h, :], eight(r_buf)[:, h, :], ACT.Exp, scale=sp[:, 8 + h:9 + h]))
                own(act.activation(eight(t2)[:, h, :], eight(r_buf)[:, h, :], ACT.Tanh, scale=sp[:, h:h + 1]),
                    "tanh_a" if h == RH - 1 else None)
            ada_row(act, 2, ps[1])
            act.wait_ge(sem("one_minus_a2"), 1)
            own(act.activation(t2, t2, ACT.Sqrt), "mult")
            ada_row(act, 3, ps[2])
            ada_columns(act, 2, ps[1])
            ada_row(act, 4, ps[3])
            ada_columns(act, 3, ps[2])
            act.wait_ge(sem("rec_out"), 1)
            own(act.activation(t1, r_buf, ACT.Square), "rec_sq")
            act.wait_ge(sem("rec_ms"), 1)
            own(act.activation(t2[:, 0:S], t2[:, 0:S], ACT.Sqrt), "rec_sqrt")
            act_hi(act, "recx", X, S, 8, 4, 8)
            ada_row(act, 5, ps[6])
            ada_columns(act, 4, ps[3])

        def pe_rec(pe):
            for g in range(2):
                ada_product(pe, g, ps[g])
            for g in range(2):
                ada_spread(pe, g, ps[g])
            pe.wait_ge(sem("cols_kept"), 2)
            pe.wait_ge(sem("xc_lo"), 1)
            w = take(pe, "gates", 0)
            wl = w[1][:, :]
            for h in range(RH):
                for g in range(2):
                    cs = slice((g * RH + h) * P, (g * RH + h + 1) * P)
                    for q, (a, b) in enumerate(((w[0][:, cs], XCo[0]), (w[0][:, cs], XCo[1]), (wl[:, cs], XCo[0]))):
                        mm = pe.matmul(ps[h][:, g * S:(g + 1) * S], a, b[:, h, :], start=q == 0, stop=q == 2)
            mm.then_inc(used, 1)
            for g, bank in ((2, 1), (3, 2), (4, 3), (5, 6)):
                pe.wait_ge(sem("gates_read"), bank + 1)
                ada_product(pe, g, ps[bank])
                if g >= 3:
                    ada_spread(pe, g - 1, ps[g - 2])
            pe.wait_ge(sem("rec_sq"), 1)
            for h in range(RH):
                mm = pe.matmul(ps[0][:, 0:S], ones, eight(t1)[:, h, :], start=h == 0, stop=h == RH - 1)
            mm.then_inc(sem("rec_sum"), 1)

        CQo = operand(S, 6, 13952)
        q_at, kv_at, k_at = 17024, 20096, 24192
        Q = at(q_at, TT * NH * QKD).rearrange("p (t h n) -> p t h n", t=TT, h=NH)
        Qf = at(q_at, TT * NH * QKD).rearrange("p (t n) -> p t n", t=TT)
        KVf = at(kv_at, TT * NH * 256).rearrange("p (t n) -> p t n", t=TT)
        KV = at(kv_at, TT * NH * 256).rearrange("p (t h n) -> p t h n", t=TT, h=NH)
        K = at(k_at, TT * NH * QKD).rearrange("p (t h n) -> p t h n", t=TT, h=NH)
        QTn, QTr, KTn, KTr = (at(27264 + i * 2048, NH * S).rearrange("p (h n) -> p h n", h=NH) for i in range(4))
        sq_tmp = at(29312, 3072)
        ATT = at(q_at, TT * NH * VD).rearrange("p (t n) -> p t n", t=TT)
        SC = at(35456, 2 * 384).rearrange("p (b n) -> p b n", b=2)
        PT = at(q_at + 2048, 2 * 384).rearrange("p (b n) -> p b n", b=2)
        ssq, rsq = cols(34), cols(32)
        krr = at(36352, 128)
        rt = at(k_at, 1024)
        mx, sums = cols(4), cols(4)
        SCALE = QKD ** -0.5

        def dve_rope(dve, own, x1, x2, cos, sin, shape):
            ts = [rt4(i, shape) for i in range(2)]
            own(dve.tensor_tensor(ts[0], x1, sin, ALU.mult))
            own(dve.tensor_tensor(ts[1], x2, sin, ALU.mult))
            own(dve.tensor_tensor(x1, x1, cos, ALU.mult))
            own(dve.tensor_tensor(x2, x2, cos, ALU.mult))
            own(dve.tensor_tensor(x1, x1, ts[1], ALU.subtract))
            own(dve.tensor_tensor(x2, x2, ts[0], ALU.add))

        def rt4(i, shape):
            n = int(np.prod(shape[1:]))
            a = rt[:, i * 512:i * 512 + n]
            return a.rearrange("p (t h n) -> p t h n", t=shape[1], h=shape[2]) if len(shape) == 4 \
                else a.rearrange("p (t n) -> p t n", t=shape[1])

        def act_attn(act, own):
            ada_columns(act, 5, ps[6])
            act_hi(act, "cq", CQo, S, 6, 2)
            for i in range(HI):
                act_part(act, BASE["uq"] + i)
            ada_row(act, 6, ps[7])
            ada_columns(act, 6, ps[7])
            for o in range(14):
                if o in (0, 2, 4, 6, 10):
                    act_part(act, BASE["uq"] + (0, 0, 1, 1, 2, 2, 3, 3, 3, 3, 4)[o] + HI)
                wait_product(act, "uq" if o < 6 else "ukv", o // 2 if o < 6 else (o - 6) // 4)
                dst = Qf[:, o % 2, (o // 2) * 512:(o // 2 + 1) * 512] if o < 6 else \
                    KVf[:, o % 2, ((o - 6) // 2) * 512:((o - 6) // 2 + 1) * 512]
                act.activation(dst, ps[o % 8][:, :], ACT.Copy).then_inc(sem("qkv_kept"), 1)
            act.wait_ge(sem("head_ms"), 1)
            own(act.activation(rsq, ssq[:, 0:32], ACT.Sqrt), "head_sqrt")
            for g in (7, 8):
                ada_row(act, g, ps[g - 1])
            for g in (7, 8):
                ada_columns(act, g, ps[g - 1])
            for i in range(HI):
                act_part(act, BASE["out"] + i)
            for b in range(8):
                act.wait_ge(sem("turned_n"), b + 1)
                dst = QTn if b < 4 else KTn
                act.activation(dst[:, 2 * (b % 4):2 * (b % 4) + 2, :], ps[(2 * b) % 8][:, :].rearrange("p (h n) -> p h n", h=2),
                               ACT.Copy).then_inc(sem("kept_n"), 1)
            for h in range(NH):
                b = h % 2
                act.wait_ge(sem("neg_max"), 2 * (h + 1))
                for t in range(TT):
                    c = slice(0, 128) if t == 0 else slice(128, 384)
                    act.activation(SC[:, b, c], SC[:, b, c], ACT.Exp, bias=mx[:, 2 * b + t:2 * b + t + 1], scale=SCALE,
                                   accum_out=sums[:, 2 * b + t:2 * b + t + 1]).then_inc(sem("probs"), 1)
                act.wait_ge(sem("probs_turned"), h + 1)
                if h >= 2:
                    act.wait_ge(sem("attn_pv"), h - 1)
                act.activation(PT[:, b, :], ps[2 + b][:, 0:384], ACT.Copy).then_inc(sem("probs_kept"), 1)
            act.wait_ge(sem("att"), 2 * NH)
            for t in range(TT):
                own(act.activation(sq_tmp[:, 0:1024], ATT[:, t, :], ACT.Square, accum_out=ss[:, t:t + 1]), "norm_ss")
            norm_wait(act, "ao", "ms", 1)
            own(act.activation(rs[:, 0:2], ss[:, 0:2], ACT.Sqrt), "norm_sqrt")
            act_hi(act, "ao", X, S, 8, 4)

        def dve_attn(dve, own):
            dve_norm(dve, own, "cq", 2, S, lambda k, j: pv("q_g", k, 1) if k < 4 else pv("kv_g", k - 4, 1), None,
                     kts=6, group=2, X=CQo)
            dve.wait_ge(sem("qkv_kept"), 14)
            sq = sq_tmp.rearrange("p (t h n) -> p t h n", t=TT, h=NH)
            own(dve.tensor_tensor(sq_tmp.rearrange("p (t n) -> p t n", t=TT), Qf, Qf, ALU.mult))
            own(dve.tensor_reduce(ssq[:, 0:16].rearrange("p (t h) -> p t h", t=TT), sq, AX.X, ALU.add))
            sqk = sq_tmp[:, 0:2048].rearrange("p (t h n) -> p t h n", t=TT, h=NH)
            own(dve.tensor_tensor(sqk, KV[:, :, :, 0:NOPE], KV[:, :, :, 0:NOPE], ALU.mult))
            own(dve.tensor_reduce(ssq[:, 16:32].rearrange("p (t h) -> p t h", t=TT), sqk, AX.X, ALU.add))
            kr = cq[:, :, QR + KVR:CQW]
            krs = krr.rearrange("p (t n) -> p t n", t=TT)
            own(dve.tensor_tensor(krs, kr, kr, ALU.mult))
            own(dve.tensor_reduce(ssq[:, 32:34], krs, AX.X, ALU.add))
            for t in range(TT):
                own(dve.tensor_scalar(ssq[:, 16 + 8 * t:24 + 8 * t], ssq[:, 16 + 8 * t:24 + 8 * t], ssq[:, 32 + t:33 + t], None, ALU.add))
            own(dve.tensor_scalar(ssq[:, 0:32], ssq[:, 0:32], 1.0 / QKD, EPS, ALU.mult, ALU.add), "head_ms")
            dve.wait_ge(sem("head_sqrt"), 1)
            own(dve.reciprocal(rsq, rsq))
            r2 = rsq.rearrange("p (a t h) -> p a t h", a=2, t=TT)
            rq = r2[:, 0].unsqueeze(3)
            rk = r2[:, 1].unsqueeze(3)
            Q3 = at(q_at, 3072).rearrange("p (a n) -> p a n", n=QKD)
            own(dve.tensor_tensor(Q, Q, rq.broadcast_to([P, TT, NH, QKD]), ALU.mult))
            own(dve.tensor_tensor(Q3, Q3, gqk[:, 0:192].unsqueeze(1).broadcast_to([P, 16, QKD]), ALU.mult))
            cos2 = cosv.rearrange("p (t n) -> p t n", t=TT)
            sin2 = sinv.rearrange("p (t n) -> p t n", t=TT)
            shape = [P, TT, NH, 32]
            dve_rope(dve, own, Q[:, :, :, NOPE:NOPE + 32], Q[:, :, :, NOPE + 32:QKD],
                     cos2.unsqueeze(2).broadcast_to(shape), sin2.unsqueeze(2).broadcast_to(shape), shape)
            dve.sem_inc(sem("q_ready"), 1)
            own(dve.tensor_tensor(krs, kr, gqk[:, 192 + NOPE:384].unsqueeze(1).broadcast_to([P, TT, ROPE]), ALU.mult))
            dve_rope(dve, own, krs[:, :, 0:32], krs[:, :, 32:64], cos2, sin2, [P, TT, 32])
            own(dve.tensor_tensor(K[:, :, :, NOPE:QKD], krs.unsqueeze(2).broadcast_to([P, TT, NH, ROPE]),
                                  rk.broadcast_to([P, TT, NH, ROPE]), ALU.mult))
            own(dve.tensor_tensor(K[:, :, :, 0:NOPE], KV[:, :, :, 0:NOPE], rk.broadcast_to([P, TT, NH, NOPE]), ALU.mult))
            K3 = at(k_at, 3072).rearrange("p (a n) -> p a n", n=QKD)
            own(dve.tensor_tensor(K3[:, :, 0:NOPE], K3[:, :, 0:NOPE],
                                  gqk[:, 192:192 + NOPE].unsqueeze(1).broadcast_to([P, 16, NOPE]), ALU.mult), "k_ready")
            for b in range(8):
                dve.wait_ge(sem("turned_r"), b + 1)
                dst = QTr if b < 4 else KTr
                dve.tensor_copy(dst[0:64, 2 * (b % 4):2 * (b % 4) + 2, :],
                                ps[(2 * b + 1) % 8][0:64, :].rearrange("p (h n) -> p h n", h=2)).then_inc(sem("kept_r"), 1)

            def scores(h):
                b = h % 2
                dve.wait_ge(sem("scores"), h + 1)
                if h >= 2:
                    dve.wait_ge(sem("probs_turned"), h - 1)
                own(dve.tensor_tensor(SC[:, b, 0:128], ps[b][:, 0:128], cn("causal"), ALU.add))
                own(dve.tensor_copy(SC[:, b, 128:256], ps[b][:, 128:256]))
                own(dve.tensor_tensor(SC[:, b, 256:384], ps[b][:, 256:384], cn("causal"), ALU.add), "scores_kept")
                own(dve.tensor_reduce(mx[:, 2 * b:2 * b + 1], SC[:, b, 0:128], AX.X, ALU.max))
                own(dve.tensor_reduce(mx[:, 2 * b + 1:2 * b + 2], SC[:, b, 128:384], AX.X, ALU.max))
                own(dve.tensor_scalar(mx[:, 2 * b:2 * b + 2], mx[:, 2 * b:2 * b + 2], -SCALE, None, ALU.mult), "neg_max")
                dve.sem_inc(sem("neg_max"), 1)

            def weighted(h):
                b = h % 2
                dve.wait_ge(sem("attn_pv"), h + 1)
                own(dve.reciprocal(sums[:, 2 * b:2 * b + 2], sums[:, 2 * b:2 * b + 2]))
                for t in range(TT):
                    own(dve.tensor_scalar(ATT[:, t, h * VD:(h + 1) * VD], ps[4 + b][:, t * VD:(t + 1) * VD],
                                          sums[:, 2 * b + t:2 * b + t + 1], None, ALU.mult), "att")
            for h in range(NH + 1):
                if h < NH:
                    scores(h)
                if h >= 1:
                    weighted(h - 1)
            for i in range(HI):
                dve_part(dve, BASE["out"] + i)
            dve_rms(dve, own, "ao", 2, 1024)
            dve_diag(dve, own, "ao", 2)
            dve_norm(dve, own, "ao", 2, S, lambda k, j: pv("attn_g", k, 1), None, kts=8, X=X)

        def pe_attn(pe):
            norm_wait(pe, "cq", "diag", 4)
            for k in range(6):
                for t in range(TT):
                    src = cq[:, t, k * P:(k + 1) * P]
                    mm = pe.matmul(ps[k][:, t * P:(t + 1) * P], src, diag[:, t + (2 if k >= 4 else 0), :], start=True, stop=True)
                mm.then_inc(sem("norm_turned"), 1)
            ada_spread(pe, 5, ps[6])
            ada_product(pe, 6, ps[7])
            ada_spread(pe, 6, ps[7])
            norm_wait(pe, "cq", "lo", 3)
            for c in range(3):
                token_product(pe, "uq", c, [(t, ps[2 * c + t][:, :]) for t in range(TT)], CQo, 4, 512, 0, True, True)
            for c in range(2):
                w = take(pe, "ukv", c)
                wl = w[1][:, :]
                for j in range(2):
                    for t in range(TT):
                        o = 6 + (2 * c + j) * 2 + t
                        if o == 7:
                            pe.wait_ge(sem("cols_kept"), 7)
                        if o >= 8:
                            pe.wait_ge(sem("qkv_kept"), o - 7)
                        for k in range(2):
                            cs = slice(k * 1024 + j * 512, k * 1024 + (j + 1) * 512)
                            for q, (a, b) in enumerate(((CQo[0], w[0]), (CQo[1], w[0]), (CQo[0], wl))):
                                mm = pe.matmul(ps[o % 8][:, :], a[:, 4 + k, t * P:(t + 1) * P], b[:, cs],
                                               start=k == 0 and q == 0, stop=k == 1 and q == 2)
                mm.then_inc(used, 1)
            for g in (7, 8):
                pe.wait_ge(sem("qkv_kept"), g)
                ada_product(pe, g, ps[g - 1])
            for g in (7, 8):
                ada_spread(pe, g, ps[g - 1])
            for b in range(8):
                src = Q if b < 4 else K
                if b == 3:
                    pe.wait_ge(sem("cols_kept"), 9)
                if b == 0:
                    pe.wait_ge(sem("q_ready"), 1)
                if b == 4:
                    pe.wait_ge(sem("k_ready"), 1)
                if b >= 4:
                    pe.wait_ge(sem("kept_n"), b - 3)
                    pe.wait_ge(sem("kept_r"), b - 3)
                for part in range(2):
                    bank = ps[(2 * b + part) % 8]
                    for j in range(2):
                        for t in range(TT):
                            h = 2 * (b % 4) + j
                            dst = bank[:, (j * 2 + t) * P:(j * 2 + t + 1) * P]
                            if part == 0:
                                mm = pe.transpose(dst, src[:, t, h, 0:NOPE], ident)
                            else:
                                mm = pe.transpose(dst[0:64, :], src[:, t, h, NOPE:QKD], ident)
                    mm.then_inc(sem("turned_r" if part else "turned_n"), 1)
            pe.wait_ge(sem("kept_n"), 8)
            pe.wait_ge(sem("kept_r"), 8)

            def scores(h):
                bank = ps[h % 2]
                if h >= 2:
                    pe.wait_ge(sem("scores_kept"), h - 1)
                for t in range(TT):
                    dst = bank[:, 0:128] if t == 0 else bank[:, 128:384]
                    n = P * (t + 1)
                    pe.matmul(dst, QTn[:, h, t * P:(t + 1) * P], KTn[:, h, 0:n], start=True, stop=False)
                    mm = pe.matmul(dst, QTr[0:64, h, t * P:(t + 1) * P], KTr[0:64, h, 0:n], start=False, stop=True)
                mm.then_inc(sem("scores"), 1)

            def weighted(h):
                b = h % 2
                pe.wait_ge(sem("probs"), 2 * (h + 1))
                if h >= 2:
                    pe.wait_ge(sem("probs_kept"), h - 1)
                for j in range(3):
                    mm = pe.transpose(ps[2 + b][:, j * P:(j + 1) * P], SC[:, b, j * P:(j + 1) * P], ident)
                mm.then_inc(sem("probs_turned"), 1)
                pe.wait_ge(sem("probs_kept"), h + 1)
                if h >= 2:
                    pe.wait_ge(sem("att"), 2 * (h - 1))
                bank = ps[4 + b]
                v = lambda t: KV[:, t, h, NOPE:256]
                pe.matmul(bank[:, 0:VD], PT[:, b, 0:128], v(0), start=True, stop=True)
                pe.matmul(bank[:, VD:2 * VD], PT[:, b, 128:256], v(0), start=True, stop=False)
                pe.matmul(bank[:, VD:2 * VD], PT[:, b, 256:384], v(1), start=False, stop=True).then_inc(sem("attn_pv"), 1)
            for h in range(NH + 1):
                if h < NH:
                    scores(h)
                if h >= 1:
                    weighted(h - 1)
            norm_wait(pe, "ao", "diag", 2)
            for k in range(8):
                for t in range(TT):
                    mm = pe.matmul(ps[k][:, t * P:(t + 1) * P], ATT[:, t, k * P:(k + 1) * P], diag[:, t, :], start=True, stop=True)
                mm.then_inc(sem("norm_turned"), 1)

        def pe_out(pe, seg, Xo, T, key, ready=None):
            for n in range(4):
                for c in range(4):
                    if n == 0 and ready:
                        ready(c)
                    if c == 0 and (n + 1) * T > 8:
                        pe.wait_ge(sem(key), (n + 1) * T - 8)
                    token_product(pe, seg, 4 * n + c, [(t, ps[(n * T + t) % 8][:, :]) for t in range(T)], Xo,
                                  4, 512, 4 * c, c == 0, c == 3)

        def act_stream(act, seg):
            for c in range(COUNT[seg]):
                act_part(act, BASE[seg] + c + HI)

        def dve_out1(dve, own):
            for n in range(4):
                for c in range(4 * n, 4 * n + 4):
                    dve_part(dve, BASE["out"] + c + HI)
                wait_product(dve, "out", 4 * n + 3)
                for t in range(TT):
                    r = res[:, t, n * 512:(n + 1) * 512]
                    dve.tensor_tensor(r, r, ps[n * TT + t][:, :], ALU.add).then_inc(sem("out1_kept"), 1)

        QO = operand(S, KT, 12288)
        scr = at(20480, 32 * KEYS).rearrange("p (s n) -> p s n", n=KEYS)
        tk, ixf = at(24576, 512), at(25600, 512)
        ix = at(25088, 512).bitcast(U32)
        cand = at(12288, 4096)
        tv, gv = at(26112, 256), at(28160, 256)
        tp = at(26368, 256).bitcast(U32)
        pij_i, pij = at(26624, 512).bitcast(U32), at(27136, 512)
        e12 = at(27648, 512)
        eq = at(20480, 4096)
        et = at(34816, 2 * S).rearrange("p (a n) -> p a n", a=2)
        gate3 = at(35328, 3 * S // 2).bitcast(BF16).rearrange("p (a n) -> p a n", a=3)
        sume = cols(16)

        def pe_query(pe):
            for c in range(KT):
                if c >= 8:
                    norm_wait(pe, "q", "full", c - 7)
                channel_product(pe, "wq", c, ps[c % 8][:, 0:S], X, S)
            norm_wait(pe, "q", "lo", 4)
            w = take(pe, "keys", 0)
            wl = w[1][:, :]
            for hh in range(16):
                cs = slice(hh * KEYS, (hh + 1) * KEYS)
                for t in range(TT):
                    k = (hh % 2) * 2 + t
                    for q, (a, b) in enumerate(((QO[0], w[0]), (QO[1], w[0]), (QO[0], wl))):
                        mm = pe.matmul(ps[hh // 2][:, k * KEYS:(k + 1) * KEYS], a[:, hh, t * P:(t + 1) * P], b[:, cs],
                                       start=q == 0, stop=q == 2)
            mm.then_inc(used, 1)

        def act_query(act, own):
            for g in range(4):
                for c in range(4 * g, 4 * g + 4):
                    act_part(act, BASE["wq"] + c + HI)
                norm_wait(act, "q", "full", 4 * (g + 1))
                ks = slice(4 * g, 4 * g + 4)
                act.activation(QO[0][:, ks, :], QO[2][:, ks, :], ACT.Copy).then_inc(sem("norm_hi"), 1)
            wait_product(act, "keys", 0)
            for b in range(0, 8, 2):
                act.activation(scr[:, 4 * b:4 * b + 4, :], ps[b][:, :].rearrange("p (k n) -> p k n", k=4),
                               ACT.Copy).then_inc(sem("scr_kept"), 1)

        def dve_query(dve, own):
            for c in range(KT):
                dve_part(dve, BASE["wq"] + c + HI)
                wait_product(dve, "wq", c)
                dve.tensor_copy(QO[2][:, c, :], ps[c % 8][:, 0:S]).then_inc(sem("norm_full"), 1)
                if c % 4 == 3 and c > 4:
                    dve_lo(dve, "q", QO, S, c // 4 - 1, 4)
            dve_lo(dve, "q", QO, S, 3, 4)
            wait_product(dve, "keys", 0)
            for b in range(1, 8, 2):
                dve.tensor_copy(scr[:, 4 * b:4 * b + 4, :], ps[b][:, :].rearrange("p (k n) -> p k n", k=4))\
                   .then_inc(sem("scr_kept"), 1)

        def top16(dve, own, rows_of):
            def step(ins_of):
                for n, row in enumerate(rows_of):
                    (own if n == len(rows_of) - 1 else own.started)(ins_of(*row))
            for r in range(2):
                e8 = slice(8 * r, 8 * r + 8)
                step(lambda values, top, where: dve.max(top[:, e8], values))
                step(lambda values, top, where: dve.max_index(where[:, e8], top[:, e8], values))
                if r == 0:
                    step(lambda values, top, where: dve.match_replace(values, top[:, e8], values, -3.0e38))

        def dve_top(dve, own):
            top16(dve, own, [(scr[:, s_, :], tk[:, 16 * s_:16 * s_ + 16], ix[:, 16 * s_:16 * s_ + 16]) for s_ in range(32)])
            own(dve.tensor_copy(ixf, ix))
            tk5 = tk.rearrange("p (h a t k) -> p h a t k", h=PH, a=2, t=TT)
            ix5 = ixf.rearrange("p (h a t k) -> p h a t k", h=PH, a=2, t=TT)
            cand5 = cand.rearrange("p (t h i j) -> p t h i j", t=TT, h=PH, i=16)
            four = [P, PH, 16, 16]
            for t in range(TT):
                own(dve.tensor_tensor(cand5[:, t], tk5[:, :, 0, t, :].unsqueeze(3).broadcast_to(four),
                                      tk5[:, :, 1, t, :].unsqueeze(2).broadcast_to(four), ALU.add))
            top16(dve, own, [(cand[:, 256 * s_:256 * s_ + 256], tv[:, 16 * s_:16 * s_ + 16], tp[:, 16 * s_:16 * s_ + 16])
                             for s_ in range(16)])
            tv3 = tv.rearrange("p (s k) -> p s k", k=16)
            gv3 = gv.rearrange("p (s k) -> p s k", k=16)
            own(dve.tensor_tensor(gv3, tv3, tv3[:, :, 0:1].broadcast_to([P, 16, 16]), ALU.subtract), "top_shifted")
            own(dve.tensor_scalar(pij_i[:, 0:256], tp, 4, None, ALU.logical_shift_right))
            own(dve.tensor_scalar(pij_i[:, 256:512], tp, 15, None, ALU.bitwise_and))
            own(dve.tensor_copy(pij, pij_i))
            eq3 = eq.rearrange("p (s j) -> p s j", j=16)
            eq5 = eq.rearrange("p (t h k j) -> p t h k j", t=TT, h=PH, k=16)
            for a in range(2):
                own(dve.tensor_tensor(eq3, cn("iota16").unsqueeze(1).broadcast_to([P, 256, 16]),
                                      pij[:, 256 * a:256 * a + 256].unsqueeze(2).broadcast_to([P, 256, 16]), ALU.is_equal))
                for t in range(TT):
                    own(dve.tensor_tensor(eq5[:, t], eq5[:, t], ix5[:, :, a, t, :].unsqueeze(2).broadcast_to(four), ALU.mult))
                own(dve.tensor_reduce(e12[:, 256 * a:256 * a + 256], eq3, AX.X, ALU.add))
            dve.wait_ge(sem("top_exp"), 1)
            own(dve.tensor_reduce(sume, gv3, AX.X, ALU.add))
            own(dve.reciprocal(sume, sume))
            own(dve.tensor_tensor(gv3, gv3, sume.unsqueeze(2).broadcast_to([P, 16, 16]), ALU.mult), "pairs_ready")
            dve.wait_ge(sem("pairs_turned"), 1)
            own(dve.tensor_copy(et[:, 0:2, :], ps[3][:, :].rearrange("p (a n) -> p a n", a=2)))
            rest = at(36096, S)
            own(dve.tensor_copy(rest, ps[6][:, 0:S]))
            for a in range(3):
                own(dve.tensor_copy(gate3[:, a, :], rest))
                if a < 2:
                    own(dve.tensor_tensor(rest, rest, gate3[:, a, :], ALU.subtract))

        gates_bc = at(28672, 3 * D).rearrange("p (g n) -> p g n", g=3)
        GATE = {(0, 0): 0, (0, 1): 1, (1, 0): 2}
        group_of = lambda name: ADA_AT.index((name, 0)) // 4
        FIRST_TOP, FIRST_GATE, FIRST_POST = group_of("ada_top"), ADA.index((0, 8)), group_of("ada_post")
        END_TOP = FIRST_GATE + 4
        ada_bank = lambda g: ps[g % 2]
        gate_banks = lambda g: (ps[4], ps[5]) if g % 2 == 0 else (ps[2], ps[7])

        def pe_ada(pe):
            pe.wait_ge(sem("scr_kept"), 8)
            for g in range(FIRST_TOP, END_TOP):
                if g == FIRST_GATE + 3:
                    pe.wait_ge(sem("pairs_ready"), 1)
                    for a in range(2):
                        for t in range(TT):
                            pe.transpose(ps[3][:, (2 * a + t) * P:(2 * a + t + 1) * P], e12[:, (2 * a + t) * P:(2 * a + t + 1) * P], ident)
                    for t in range(TT):
                        mm = pe.transpose(ps[6][:, t * P:(t + 1) * P], gv[:, t * P:(t + 1) * P], ident)
                    mm.then_inc(sem("pairs_turned"), 1)
                if g >= FIRST_TOP + 2:
                    pe.wait_ge(sem("row_kept"), g - 1)
                    columns_kept(pe, g - 1)
                ada_product(pe, g, ada_bank(g))
                if g > FIRST_TOP:
                    spread(pe, g - 1)
            spread(pe, END_TOP - 1)

        def spread(pe, g):
            if g < FIRST_GATE:
                return ada_spread(pe, g, ada_bank(g))
            pe.wait_ge(sem("row_kept"), g + 1)
            if g >= FIRST_GATE + 2:
                pe.wait_ge(sem("gate_kept"), g - FIRST_GATE - 1)
            row = rows[0:2, g % 2, :]
            lat, ctx_ = gate_banks(g)
            pe.matmul(lat[:, :], cn("sel_lat")[0:2, :], row, start=True, stop=True)
            pe.matmul(ctx_[:, :], cn("sel_ctx")[0:2, :], row, start=True, stop=True).then_inc(sem("spread"), 1)

        def act_top(act, own):
            gate_in = sem("gates_in")
            for k in range(2):
                act.dma_start(gates_bc[:, k, :], d["ada_b_gate"][0:1, :].broadcast_to([P, D])).then_inc(gate_in, 16)
            for g in range(FIRST_TOP, END_TOP):
                ada_row(act, g, ada_bank(g))
                if FIRST_TOP < g <= FIRST_GATE:
                    ada_columns(act, g - 1, ada_bank(g - 1))
                if g == FIRST_GATE + 1:
                    act.wait_ge(sem("top_shifted"), 1)
                    own(act.activation(gv, gv, ACT.Exp), "top_exp")

        def gate_kept(dve, own, g, gs):
            dve.wait_ge(sem("spread"), g + 1)
            for k, bank in ((0, gate_banks(g)[0]), (1, gate_banks(g)[1])):
                gate = gates_bc[:, k, gs]
                own(dve.tensor_tensor(gate, gate, bank[:, :], ALU.add), "gate_kept" if k else None)

        def final_columns(dve, own, layer):
            a3 = ada_cols[:, 64 * layer:64 * layer + 64].rearrange("p (k s) -> p k s", s=2)
            bias = pv("ada_b")[:, 32 * layer:32 * layer + 32]
            own(dve.tensor_tensor(a3, a3, bias.unsqueeze(2).broadcast_to([P, 32, 2]), ALU.add))
            own(dve.tensor_scalar(a3[:, 16:32, :], a3[:, 16:32, :], 1.0, None, ALU.add))
            own(dve.tensor_tensor(a3[:, 16:32, :], a3[:, 16:32, :],
                                  pv("pre_g")[:, 16 * layer:16 * layer + 16].unsqueeze(2).broadcast_to([P, 16, 2]), ALU.mult))

        def dve_ada(dve, own):
            dve.wait_ge(sem("gates_in"), 32)
            for n in range(4):
                gate_kept(dve, own, FIRST_GATE + n, slice(n * 512, (n + 1) * 512))
            columns_kept(dve, FIRST_GATE)
            final_columns(dve, own, 0)

        G = at(12288, HALF * S).rearrange("p (i t) -> p i t", i=HALF)
        Gf = at(12288, HALF * S)
        BATCH, HOTS = 4, 4
        BY_POOL = BATCH - 1
        hot2 = [a.bitcast(BF16).rearrange("p (t n) -> p t n", t=BATCH) for a in
                (diag_at[:, 0:256], diag_at[:, 256:512], gqk_sb[:, 0:256], at(37248, 256))]
        hot1 = at(35712, 1536).bitcast(BF16).rearrange("p (b t a n) -> p b t a n", b=HOTS, t=BATCH, a=3)
        bare = at(37504, 384).bitcast(BF16).rearrange("p (b t n) -> p b t n", b=HOTS, t=BY_POOL)
        BATCHES, BANKS = S // BATCH, 4
        rows_g = at(32768, 1024).rearrange("p (b n) -> p b n", b=2)
        PEELED = TURN = 8

        def batches(eng, part, half):
            for n in range(PEELED):
                part(n, None)
            with eng.Fori(0, (BATCHES - PEELED) // TURN) as j:
                for n in range(PEELED, PEELED + TURN):
                    part(n, j)

        def batch_wait(eng, name, half, n, j):
            v = half * BATCHES + n
            eng.wait_ge(sem(name), v if j is None else j * TURN + v)

        def dve_gates(dve, own, half):
            def part(n, j):
                b = n % HOTS
                if half * BATCHES + n >= HOTS:
                    batch_wait(dve, "dense_mm", half, n - HOTS + 1, j)
                first = n * BATCH if j is None else j * (TURN * BATCH) + n * BATCH
                tokens = lambda k, m: slice(first + k, first + k + m) if j is None else bass.ds(first + k, m)
                iota1 = cn("iota")[:, half * HALF:(half + 1) * HALF].unsqueeze(1)
                shape = [P, BY_POOL, HALF]
                dve.tensor_tensor(bare[:, b], iota1.broadcast_to(shape),
                                  et[:, 0, tokens(0, BY_POOL)].unsqueeze(2).broadcast_to(shape), ALU.is_equal).then_inc(sem("bare"), 1)
                shape = [P, BATCH, KEYS]
                dve.tensor_tensor(hot2[b], cn("iota").unsqueeze(1).broadcast_to(shape),
                                  et[:, 1, tokens(0, BATCH)].unsqueeze(2).broadcast_to(shape), ALU.is_equal)
                last = tokens(BY_POOL, 1)
                dve.scalar_tensor_tensor(hot1[:, b, BY_POOL], iota1.broadcast_to([P, 3, HALF]), et[:, 0, last],
                                         gate3[:, :, last].broadcast_to([P, 3, HALF]),
                                         ALU.is_equal, ALU.mult).then_inc(sem("hot"), 1)
            batches(dve, part, half)
            for i in range(HI):
                dve_part(dve, BASE[f"u{half}"] + i)

        def pool_gates(pool, half):
            def part(n, j):
                b = n % HOTS
                batch_wait(pool, "bare", half, n + 1, j)
                tokens = slice(n * BATCH, n * BATCH + BY_POOL) if j is None else bass.ds(j * (TURN * BATCH) + n * BATCH, BY_POOL)
                shape = [P, BY_POOL, 3, HALF]
                pool.tensor_tensor(hot1[:, b, 0:BY_POOL], bare[:, b].unsqueeze(2).broadcast_to(shape),
                                   gate3[:, :, tokens].rearrange("p a t -> p t a").unsqueeze(3).broadcast_to(shape),
                                   ALU.mult).then_inc(sem("hot_gated"), 1)
            batches(pool, part, half)

        def pe_gates(pe, half):
            def part(n, j):
                if half * BATCHES + n >= BANKS:
                    batch_wait(pe, "dense_kept", half, n - BANKS + 1, j)
                batch_wait(pe, "hot", half, n + 1, j)
                batch_wait(pe, "hot_gated", half, n + 1, j)
                for t in range(BATCH):
                    for a in range(3):
                        mm = pe.matmul(ps[n % BANKS][:, t * HALF:(t + 1) * HALF], hot2[n % HOTS][:, t],
                                       hot1[:, n % HOTS, t, a], start=a == 0, stop=a == 2)
                mm.then_inc(sem("dense_mm"), 1)
            g0 = group_of(f"ada_g{half}")
            for n in range(BATCHES):
                part(n, None)
                c, at_end = divmod(n, 6)
                if at_end == 5 and c < 8:
                    ada_product(pe, g0 + c // 4, ps[BANKS + c // 4], (c % 4,))
            for g in range(2):
                ada_spread(pe, g0 + g, ps[BANKS + g], rows_g)

        def act_gates(act, own, half):
            def part(n, j):
                batch_wait(act, "dense_mm", half, n + 1, j)
                to = slice(n * BATCH, (n + 1) * BATCH) if j is None else bass.ds(j * (TURN * BATCH) + n * BATCH, BATCH)
                act.activation(G[:, :, to].rearrange("p i t -> p t i"),
                               ps[n % BANKS][:, 0:BATCH * HALF].rearrange("p (t i) -> p t i", t=BATCH),
                               ACT.Copy).then_inc(sem("dense_kept"), 1)
            with act.Fori(0, BATCHES // TURN - 1) as j:
                for n in range(TURN):
                    part(n, j)
            g0 = group_of(f"ada_g{half}")
            for g in range(2):
                ada_row(act, g0 + g, ps[BANKS + g], rows_g)
            for i in range(HI):
                act_part(act, BASE[f"u{half}"] + i)
            for n in range(BATCHES - TURN, BATCHES):
                part(n, None)
            for g in range(2):
                ada_columns(act, g0 + g, ps[BANKS + g])

        gel = at(36352, 512).rearrange("p (b n) -> p b n", b=2)
        wpart = at_r(36864, 1024).rearrange("p (b a n) -> p b a n", b=2, a=2)
        LOOPS = HALF // RAW

        def looped(eng, turn):
            turn(None, 0)
            with eng.Fori(1, LOOPS - 1) as j:
                turn(j, None)
            turn(None, LOOPS - 1)

        def value(j, py, per, base):
            return j * per + base if py is None else py * per + base

        def pe_u(pe, half):
            def turn(j, py):
                for r in range(RAW):
                    n = half * HALF + r
                    if py != 0 or n >= 4:
                        pe.wait_ge(sem("gelu"), value(j, py, RAW, n - 3))
                    c = r if py is None else RAW * py + r
                    channel_product(pe, f"u{half}", c, ps[r][:, 0:S], X, S, j, RAW if py is None else 0)
            looped(pe, turn)

        def act_u(act, own, half):
            base = BASE[f"u{half}"]
            def turn(j, py):
                for r in range(RAW):
                    n = half * HALF + r
                    i = base + (r if py is None else RAW * py + r)
                    act.wait_ge(used, value(j, py, RAW, base + r + 1))
                    act_part(act, i + HI, j, RAW if py is None else 0)
                    if py != 0 or n >= 2:
                        act.wait_ge(sem("gated"), value(j, py, RAW, n - 1))
                    act.activation(gel[:, r % 2, :], ps[r][:, 0:S], ACT.Gelu).then_inc(sem("gelu"), 1)
            looped(act, turn)

        def dve_u(dve, own, half):
            base = BASE[f"u{half}"]
            def turn(j, py):
                for r in range(RAW):
                    i = base + (r if py is None else RAW * py + r)
                    dve_part(dve, i + HI, j, RAW if py is None else 0)
                    dve.wait_ge(sem("gelu"), value(j, py, RAW, half * HALF + r + 1))
                    g = Gf[:, bass.ds(j * (RAW * S) + r * S, S)] if py is None else Gf[:, (RAW * py + r) * S:(RAW * py + r + 1) * S]
                    dve.tensor_tensor(g, g, gel[:, r % 2, :], ALU.mult).then_inc(sem("gated"), 1)
            looped(dve, turn)

        def pe_v(pe, half):
            seg = f"v{half}"
            def turn(j, py):
                for r in range(RAW):
                    c = r if py is None else RAW * py + r
                    whi, wlo = take(pe, seg, c, j, RAW if py is None else 0)
                    wl = wlo[:, :]
                    pe.wait_ge(sem("w_lo"), value(j, py, RAW, half * HALF + r + 1))
                    xh, xl = (wpart[:, r % 2, a, :] for a in range(2))
                    for t in range(TT):
                        for n in range(4):
                            ns, ts = slice(n * 512, (n + 1) * 512), slice(t * P, (t + 1) * P)
                            for q, (a, b) in enumerate(((xh, whi), (xl, whi), (xh, wl))):
                                mm = pe.matmul(ps[4 * t + n][:, :], a[:, ts], b[:, ns], start=py == 0 and r == 0 and q == 0,
                                               stop=py == LOOPS - 1 and r == RAW - 1 and q == 2, skip_group_check=True)
                    mm.then_inc(used, 1)
            looped(pe, turn)

        def v_source(j, py, tile):
            return Gf[:, bass.ds(j * (RAW * S) + tile * S, S)] if py is None else Gf[:, tile * S:(tile + 1) * S]

        def act_v(act, own, half):
            base = BASE[f"v{half}"]
            def w_hi(j, py, r, c):
                act.activation(wpart[:, r % 2, 0, :], v_source(j, py, c), ACT.Copy).then_inc(sem("w_hi"), 1)
            w_hi(None, 0, 0, 0)
            w_hi(None, 0, 1, 1)
            def turn(j, py):
                for r in range(RAW):
                    c = r if py is None else RAW * py + r
                    act.wait_ge(used, value(j, py, RAW, base + r + 1))
                    act_part(act, base + c + HI, j, RAW if py is None else 0)
                    if c + 2 < HALF:
                        w_hi(j, py, r, c + 2)
            looped(act, turn)

        def dve_v(dve, own, half):
            base = BASE[f"v{half}"]
            def w_lo(j, py, r, c, n):
                dve.wait_ge(sem("w_hi"), value(j, py, RAW, n) if j is not None else n)
                dve.tensor_tensor(wpart[:, r % 2, 1, :], v_source(j, py, c), wpart[:, r % 2, 0, :].bitcast(F32),
                                  ALU.subtract).then_inc(sem("w_lo"), 1)
            w_lo(None, 0, 0, 0, half * HALF + 1)
            w_lo(None, 0, 1, 1, half * HALF + 2)
            def turn(j, py):
                for r in range(RAW):
                    c = r if py is None else RAW * py + r
                    dve_part(dve, base + c + HI, j, RAW if py is None else 0)
                    if c + 2 < HALF:
                        w_lo(j, py, r, c + 2, half * HALF + c + 3)
            looped(dve, turn)
            wait_product(dve, f"v{half}", HALF - 1)
            for t in range(TT):
                for n in range(4):
                    r = res[:, t, n * 512:(n + 1) * 512]
                    dve.tensor_tensor(r, r, ps[4 * t + n][:, :], ALU.add).then_inc(sem("experts_kept"), 1)

        N2 = 2 * S
        X2 = operand(N2)
        ctx_res = at(20480, TT * D).rearrange("p (t d) -> p t d", t=TT)
        both_tiles = [lambda k, t=t: (res if t < 2 else ctx_res)[:, t % 2, k * P:(k + 1) * P] for t in range(4)]
        a4 = ada_cols.rearrange("p (l k s) -> p l k s", l=2, s=2)
        SPAN = ((0, S, 0), (S, N2, 1))
        mix = at(20480, KT * N2).rearrange("p (k n) -> p k n", k=KT)
        pooled_hi = at_r(0, 8 * N2).rearrange("p (k n) -> p k n", k=8)
        pooled_lo = at_r(20480, 8 * N2).rearrange("p (k n) -> p k n", k=8)
        vs = at(34816, 1024).rearrange("p (b n) -> p b n", b=2)
        PADW = 4 * 80 + S + 16
        pads = at(35840, 2 * PADW).rearrange("p (b n) -> p b n", b=2)
        rcount = at(37024, N2)

        def act_n3(act, own):
            act.dma_start(ctx_res, d["ctx"].rearrange("(t p) d -> p t d", p=P)).then_inc(sem("ctx_in"), 16)
            act.dma_start(scratch, at(0, TT * D)).then_inc(sem("spilled"), 16)
            act.dma_start(gates_bc[:, 2, :], d["ada_b_gate"][1:2, :].broadcast_to([P, D])).then_inc(sem("gates_in"), 16)
            act_norm(act, own, "n3", [(res if t < 2 else ctx_res)[:, t % 2, :] for t in range(4)], N2,
                     arrived=lambda: act.wait_ge(sem("ctx_in"), 16))
            act.wait_ge(sem("spilled"), 16)

        def modulated(layer):
            return (lambda k, j: a4[:, layer, 16 + k, j:j + 1]), (lambda k, j: a4[:, layer, k, j:j + 1])

        def dve_n3(dve, own):
            dve_rms(dve, own, "n3", 4)
            dve_diag(dve, own, "n3", 4)
            dve_norm(dve, own, "n3", 4, N2, *modulated(0), span=SPAN)

        def pe_even(pe):
            for c in range(8):
                channel_product(pe, "ev_a", c, ps[c][:, :], X2, N2)
            w = take(pe, "pool", 0)
            wl = w[1][:, :]
            pe.wait_ge(sem("a_kept"), 8)
            for g in range(4):
                pe.wait_ge(sem("pool_lo"), 2 * g + 2)
                for o in range(2):
                    for k in range(2):
                        cs = slice((g * 2 + k) * 256 + o * P, (g * 2 + k) * 256 + (o + 1) * P)
                        for q, (a, b) in enumerate(((w[0][:, cs], pooled_hi), (w[0][:, cs], pooled_lo), (wl[:, cs], pooled_hi))):
                            mm = pe.matmul(ps[2 * g + o][:, :], a, b[:, 2 * g + k, :], start=k == 0 and q == 0,
                                           stop=k == 1 and q == 2)
            mm.then_inc(used, 1)
            for c in range(40):
                if c < 8:
                    pe.wait_ge(sem("mixed_kept"), c + 1)
                elif c < 16:
                    pe.wait_ge(sem("a_done"), c - 7)
                else:
                    pe.wait_ge(sem("b_done"), (c - 8) // 4 - 1)
                channel_product(pe, "ev_b", c, ps[c % 8][:, :], X2, N2)

        def act_even(act, own):
            for c in range(8):
                if c % 2 == 0:
                    if c:
                        act.wait_ge(sem("pool_full"), c)
                    act.dma_start(rcount, d["tables"][:, c * S:(c + 2) * S]).then_inc(sem("tables_in"), 16)
                act_part(act, BASE["ev_a"] + c + HI)
                wait_product(act, "ev_a", c)
                if c >= 2:
                    act.wait_ge(sem("pool_full"), c - 1)
                act.activation(vs[:, c % 2, :], ps[c][:, :], ACT.Copy).then_inc(sem("a_kept"), 1)
                if c >= 1:
                    pooled_hi_part(act, c - 1)
            pooled_hi_part(act, 7)
            act_part(act, BASE["pool"] + HI)
            for c in range(8):
                act_part(act, BASE["ev_b"] + c + HI)
                wait_product(act, "ev_b", c)
                if c >= 2:
                    act.wait_ge(sem("a_done"), c - 1)
                act.activation(vs[:, c % 2, :], ps[c][:, :], ACT.Silu).then_inc(sem("a_silu"), 1)
            for j in range(8):
                for q in range(4):
                    c = 8 + 4 * j + q
                    act_part(act, BASE["ev_b"] + c + HI)
                    wait_product(act, "ev_b", c)
                    if q == 0:
                        if j >= 1:
                            act.wait_ge(sem("u_made"), j)
                        act.activation(bx, ps[c % 8][:, :], ACT.Copy).then_inc(sem("bx_kept"), 1)
                    if q == 3:
                        if j >= 1:
                            act.wait_ge(sem("b_done"), j)
                        act.activation(bg, ps[c % 8][:, :], ACT.Silu).then_inc(sem("bg_silu"), 1)

        def pooled_hi_part(act, c):
            act.wait_ge(sem("pool_full"), c + 1)
            act.activation(pooled_hi[:, c, :], mix[:, c, :], ACT.Copy).then_inc(sem("pool_hi"), 1)

        bx, bg, conv = at(0, N2), at(N2, N2), at(2 * N2, N2)
        up = at(3 * N2, 2 * (S + 2)).rearrange("p (s n) -> p s n", s=2)

        def dve_even(dve, own):
            dve.wait_ge(sem("tables_in"), 16)
            for c in range(8):
                w = WINDOWS[c // 2]
                if c % 2 == 0 and c:
                    dve.wait_ge(sem("tables_in"), 16 * (c // 2 + 1))
                b0, b1 = pads[:, 0, :], pads[:, 1, :]
                own(dve.memset(b0, 0.0))
                dve.wait_ge(sem("a_kept"), c + 1)
                v = vs[:, c % 2, :]
                grid = v[:, 0:S].rearrange("p (r n) -> p r n", r=4)
                rows_ = b0[:, 0:320].rearrange("p (r n) -> p r n", r=4)[:, :, 8:8 + GRID_W]
                tmp = b1[:, 0:3 * GRID_W].rearrange("p (r n) -> p r n", r=3)
                if w == 2:
                    own(dve.tensor_copy(rows_[:, 0:1], grid[:, 0:1]))
                    own(dve.tensor_tensor(rows_[:, 1:4], grid[:, 1:4], grid[:, 0:3], ALU.add))
                elif w == 4:
                    own(dve.tensor_tensor(tmp, grid[:, 0:3], grid[:, 1:4], ALU.add))
                    own(dve.tensor_copy(rows_[:, 0:1], tmp[:, 0:1]))
                    own(dve.tensor_tensor(rows_[:, 1:2], tmp[:, 0:1], grid[:, 2:3], ALU.add))
                    own(dve.tensor_tensor(rows_[:, 2:3], tmp[:, 0:1], tmp[:, 2:3], ALU.add))
                    own(dve.tensor_tensor(rows_[:, 3:4], grid[:, 1:2], tmp[:, 2:3], ALU.add))
                else:
                    own(dve.tensor_tensor(tmp[:, 0:2], grid[:, 0:2], grid[:, 2:4], ALU.add))
                    own(dve.tensor_tensor(tmp[:, 2:3], tmp[:, 0:1], tmp[:, 1:2], ALU.add))
                    own(dve.tensor_copy(rows_, tmp[:, 2:3].broadcast_to([P, 4, GRID_W])))
                own(dve.tensor_copy(b0[:, 328:328 + S], v[:, S:N2]))
                src, dst, width, step = b0, b1, PADW, 1
                while step < w:
                    width -= step
                    own(dve.tensor_tensor(dst[:, 0:width], src[:, 0:width], src[:, step:step + width], ALU.add))
                    src, dst, step = dst, src, 2 * step
                m = mix[:, c, :]
                o = 8 - w // 2
                own(dve.tensor_tensor(m[:, 0:S].rearrange("p (r n) -> p r n", r=4),
                                      src[:, 0:320].rearrange("p (r n) -> p r n", r=4)[:, :, o:o + GRID_W],
                                      rcount[:, 0:S].rearrange("p (r n) -> p r n", r=4), ALU.mult))
                own(dve.tensor_tensor(m[:, S:N2], src[:, 320 + o:320 + o + S], rcount[:, S:N2], ALU.mult))
                own(dve.tensor_tensor(m, m, v, ALU.subtract), "pool_full")
                if c >= 1:
                    pooled_lo_part(dve, c - 1)
            pooled_lo_part(dve, 7)
            wait_product(dve, "pool", 0)
            for c in range(8):
                own(dve.tensor_scalar(mix[:, c, :], ps[c][:, :], pv("pool_scale", c, 1), None, ALU.mult), "mixed_kept")
            own(dve.memset(up[:, :, 0:1], 0.0))
            own(dve.memset(up[:, :, S + 1:S + 2], 0.0))
            for c in range(8):
                dve.wait_ge(sem("a_silu"), c + 1)
                own(dve.tensor_tensor(mix[:, c, :], mix[:, c, :], vs[:, c % 2, :], ALU.mult), "a_done")
            two = lambda a: a.rearrange("p (s n) -> p s n", s=2)
            for j in range(8):
                bank = lambda q: ps[(8 + 4 * j + q) % 8][:, :]
                dve.wait_ge(sem("bx_kept"), j + 1)
                wait_product(dve, "ev_b", 8 + 4 * j + 1)
                own(dve.tensor_tensor(up[:, :, 1:S + 1], two(bank(1)), two(bx), ALU.mult), "u_made")
                own(dve.tensor_scalar(two(conv), up[:, :, 0:S], pv("conv2_w", j, 1), pv("conv2_b", j, 1), ALU.mult, ALU.add))
                for t in range(1, 3):
                    own(dve.scalar_tensor_tensor(two(conv), up[:, :, t:t + S], pv("conv2_w", 8 * t + j, 1), two(conv), ALU.mult, ALU.add))
                wait_product(dve, "ev_b", 8 + 4 * j + 2)
                own(dve.tensor_tensor(conv, conv, bank(2), ALU.mult))
                dve.wait_ge(sem("bg_silu"), j + 1)
                own(dve.tensor_tensor(mix[:, 8 + j, :], conv, bg, ALU.mult), "b_done")

        def pooled_lo_part(dve, c):
            dve.wait_ge(sem("pool_hi"), c + 1)
            dve.tensor_tensor(pooled_lo[:, c, :], mix[:, c, :], pooled_hi[:, c, :].bitcast(F32),
                              ALU.subtract).then_inc(sem("pool_lo"), 1)

        def act_masks(act):
            act.dma_start(segmask, d["tables"][:, 8 * S:10 * S]).then_inc(sem("masks_in"), 16)
            for z in range(2):
                act.dma_start(gqk_sb[:, P * z:P * (z + 1)], d["tables"][:, 10 * S + P * z:10 * S + P * (z + 1)])\
                   .then_inc(sem("masks_in"), 16)

        Y = at(20480, 4 * D).rearrange("p (t d) -> p t d", t=4)
        ctx2 = at(6144, TT * D).rearrange("p (t d) -> p t d", t=TT)

        def act_mix(act, own):
            for g in range(4):
                act.activation(X2[0][:, 4 * g:4 * g + 4, :], mix[:, 4 * g:4 * g + 4, :], ACT.Copy).then_inc(sem("mix_hi"), 1)
            act_stream(act, "ev_out")

        def dve_mix(dve, own):
            for g in range(4):
                dve.wait_ge(sem("mix_hi"), g + 1)
                own(dve.tensor_tensor(X2[1][:, 4 * g:4 * g + 4, :], mix[:, 4 * g:4 * g + 4, :],
                                  X2[0][:, 4 * g:4 * g + 4, :].bitcast(F32), ALU.subtract), "mix_lo")
            for n in range(4):
                wait_product(dve, "ev_out", 4 * n + 3)
                for t in range(4):
                    dve.tensor_copy(Y[:, t, n * 512:(n + 1) * 512], ps[(4 * n + t) % 8][:, :]).then_inc(sem("y0_kept"), 1)

        def pe_mix(pe):
            pe_out(pe, "ev_out", X2, 4, "y0_kept", lambda c: pe.wait_ge(sem("mix_lo"), c + 1))

        def post_loads(act, key, layer):
            act.dma_start(post_at(layer), d["post_g"][layer:layer + 1, :].broadcast_to([P, D])).then_inc(sem(key + "_in"), 16)
            act.dma_start(at(0, TT * D), scratch).then_inc(sem(key + "_in"), 16)

        def act_post(act, own, key, layer, T):
            if layer == 0:
                post_loads(act, key, layer)
                act.dma_start(ctx2, d["ctx"].rearrange("(t p) d -> p t d", p=P)).then_inc(sem(key + "_in"), 16)
            for t in range(T):
                own(act.activation(junk, Y[:, t, :], ACT.Square, accum_out=ss[:, t:t + 1]), "norm_ss")
            norm_wait(act, key, "ms", 1)
            own(act.activation(rs[:, 0:T], ss[:, 0:T], ACT.Sqrt), "norm_sqrt")
            if layer == 1:
                for t in range(T):
                    act.wait_ge(sem(key + "_done"), t + 1)
                    act.dma_start(out[t * P:(t + 1) * P, :], res[:, t, :]).then_inc(sem("stored"), 16)
                act.wait_ge(sem("stored"), 16 * T)
            else:
                for g in range(FIRST_POST, len(ADA)):
                    ada_row(act, g, ps[g - FIRST_POST])
                for i in range(HI):
                    act_part(act, BASE["od_v"] + i)

        def pe_post(pe):
            for g in range(FIRST_POST, len(ADA)):
                ada_product(pe, g, ps[g - FIRST_POST])
                if g > FIRST_POST:
                    spread_gate(pe, g - 1)
            spread_gate(pe, len(ADA) - 1)

        def spread_gate(pe, g):
            pe.wait_ge(sem("row_kept"), g + 1)
            pe.matmul(ps[4 + g - FIRST_POST][:, :], cn("sel_lat")[0:2, :], rows[0:2, g % 2, :],
                      start=True, stop=True).then_inc(sem("spread"), 1)

        def post_at(layer):
            return at(4096, D) if layer == 0 else at(24576, D)

        def post_gates(dve, own, key, layer):
            dve.wait_ge(sem(key + "_in"), 48 if layer == 0 else 32)
            for k in ((0, 1) if layer == 0 else (2,)):
                own(dve.tensor_tensor(gates_bc[:, k, :], gates_bc[:, k, :], post_at(layer), ALU.mult))

        def dve_post(dve, own, key, layer, T):
            if layer == 0:
                post_gates(dve, own, key, layer)
            dve_rms(dve, own, key, T)
            for t in range(T):
                g = gates_bc[:, (t // 2) if layer == 0 else 2, :]
                own(dve.scalar_tensor_tensor(Y[:, t, :], Y[:, t, :], rs[:, t:t + 1], g, ALU.mult, ALU.mult))
                x_ = res[:, t, :] if t < 2 else ctx2[:, t - 2, :]
                dst = res[:, t, :] if t < 2 else Y[:, t, :]
                own(dve.tensor_tensor(dst, x_, Y[:, t, :], ALU.add), key + "_done")

        ctx3 = at(24576, TT * D).rearrange("p (t d) -> p t d", t=TT)
        l1_tiles = [lambda k, t=t: (res if t < 2 else ctx3)[:, t % 2, k * P:(k + 1) * P] for t in range(4)]

        def act_n4(act, own):
            act.dma_start(scratch, at(0, TT * D)).then_inc(sem("spilled"), 16)
            act_norm(act, own, "n4", [(res if t < 2 else ctx3)[:, t % 2, :] for t in range(4)], N2)
            act.wait_ge(sem("spilled"), 32)

        def dve_n4(dve, own):
            dve.wait_ge(sem("spread"), len(ADA))
            dve.wait_ge(sem("gates_in"), 48)
            for n in range(4):
                gate = gates_bc[:, 2, n * 512:(n + 1) * 512]
                own(dve.tensor_tensor(gate, gate, ps[4 + n][:, :], ALU.add))
            columns_kept(dve, len(ADA))
            final_columns(dve, own, 1)
            dve_rms(dve, own, "n4", 4)
            dve_diag(dve, own, "n4", 4)
            dve_norm(dve, own, "n4", 4, N2, *modulated(1), span=SPAN)

        V = at(20480, 4 * D).rearrange("p (t d) -> p t d", t=4)

        def act_values(act, own):
            act_n4(act, own)
            act_part(act, BASE["od_v"] + HI)
            act_masks(act)
            for c in range(1, 16):
                act_part(act, BASE["od_v"] + c + HI)

        def pe_values(pe):
            pe_norm(pe, "n4", l1_tiles)
            norm_wait(pe, "n4", "full", KT)
            pe_out(pe, "od_v", X2, 4, "v_kept", lambda c: norm_wait(pe, "n4", "lo", c + 1))

        def dve_values(dve, own):
            for n in range(4):
                wait_product(dve, "od_v", 4 * n + 3)
                for t in range(4):
                    dve.tensor_copy(V[:, t, n * 512:(n + 1) * 512], ps[(4 * n + t) % 8][:, :]).then_inc(sem("v_kept"), 1)

        def dir_bufs(z):
            o = 1792 * z
            return at(o, 512), at(o + 512, 512), at(o + 1024, 512), at(o + 1536, 256)
        qbuf, gbuf = at(3584, 256), at(3840, 256)
        kdT = [at(34816 + 512 * z, 512) for z in range(2)]
        states = [at(35840 + 512 * z, 512).rearrange("p (n v) -> p n v", n=4) for z in range(2)]
        scT = [at(36864 + 256 * z, 256) for z in range(2)]
        qd = [at(37376 + 256 * z, 256) for z in range(2)]
        osq, orms = at(35328, 256), at(35584, 256)
        segmask = diag_at[:, :]
        cmask = [gqk_sb[:, P * z:P * (z + 1)].bitcast(I32) for z in range(2)]
        OT = at(28672, HG * S).rearrange("p (h n) -> p h n", h=HG)
        decay = [cols(8) for _ in range(2)]
        blast = [cols(8) for _ in range(2)]
        oml_c = omlb
        NC2 = N2 // CH

        def chunk_end(a, z):
            return a.rearrange("p (c n) -> p c n", n=CH)[:, :, CH - 1 if z == 0 else 0]

        def order(z, n=4):
            return range(n) if z == 0 else range(n - 1, -1, -1)

        def pe_small(pe, h, z):
            A, B, C, KI = dir_bufs(z)
            pe.wait_ge(sem(f"decayed{z}"), h + 1)
            if z == 1 or h >= 1:
                pe.wait_ge(sem("kdt_kept"), 2 * h + z)
            for t in range(4):
                mm = pe.transpose(ps[3][:, t * P:(t + 1) * P], C[:, t * P:(t + 1) * P], ident)
            mm.then_inc(sem("kd_turned"), 1)
            if z == 1 or h >= 1:
                pe.wait_ge(sem("masked"), 2 * h + z)
            for t in range(TT):
                mm = pe.matmul(ps[6][:, (2 * z + t) * P:(2 * z + t + 1) * P], KI[:, t * P:(t + 1) * P],
                               qd[z][:, t * P:(t + 1) * P], start=True, stop=True)
            mm.then_inc(sem("scored"), 1)
            pe.wait_ge(sem("kdt_kept"), 2 * h + z + 1)
            if z == 1 or h >= 1:
                pe.wait_ge(sem("states_done"), 2 * h + z)
            for c in range(NC2):
                rows_ = slice((c % 2) * CH, (c % 2 + 1) * CH)
                mm = pe.matmul(ps[4 + c % 2][:, (c // 2) * P:(c // 2 + 1) * P],
                               kdT[z][rows_, (c // 2) * P:(c // 2 + 1) * P],
                               V[rows_, c // 2, h * P:(h + 1) * P], start=True, stop=True)
            mm.then_inc(sem("increments"), 1)

        def pe_output(pe, h):
            pe.wait_ge(sem("masked"), 2 * h + 2)
            pe.wait_ge(sem("states_done"), 2 * h + 2)
            if h >= 1:
                pe.wait_ge(sem("head_done"), h)
            for t in range(TT):
                ts = slice(t * P, (t + 1) * P)
                pe.matmul(ps[7][:, ts], V[:, t, h * P:(h + 1) * P], scT[0][:, ts], start=True, stop=False)
                for z in range(2):
                    for c in (2 * t, 2 * t + 1):
                        cs = slice(c * CH, (c + 1) * CH)
                        pe.matmul(ps[7][:, cs], states[z][:, c, :], qd[z][:, cs], start=False,
                                  stop=False, skip_group_check=True)
                mm = pe.matmul(ps[7][:, ts], V[:, t, h * P:(h + 1) * P], scT[1][:, ts], start=False, stop=True)
            mm.then_inc(sem("o_done"), 1)

        def pe_sum(pe, h):
            pe.wait_ge(sem("o_squared"), h + 1)
            pe.matmul(ps[7][:, S:N2], ones, osq, start=True, stop=True).then_inc(sem("o_summed"), 1)

        def pe_heads(pe):
            for h in range(HG + 1):
                if h < HG:
                    if h >= 1:
                        pe.wait_ge(sem("z_kept0"), h)
                    channel_product(pe, "od_heads", 4 * h, ps[0][:, :], X2, N2)
                if h >= 1:
                    pe_small(pe, h - 1, 0)
                if h < HG:
                    if h >= 1:
                        pe.wait_ge(sem("z_kept1"), h)
                    channel_product(pe, "od_heads", 4 * h + 1, ps[1][:, :], X2, N2)
                if h >= 1:
                    pe_small(pe, h - 1, 1)
                if h < HG:
                    if h >= 1:
                        pe.wait_ge(sem("qg_kept"), 2 * h)
                    channel_product(pe, "od_heads", 4 * h + 2, ps[2][:, 0:S], X2, S)
                if h >= 1:
                    pe_output(pe, h - 1)
                if h < HG:
                    channel_product(pe, "od_heads", 4 * h + 3, ps[2][:, S:N2], X2, S)
                if h >= 1:
                    pe_sum(pe, h - 1)

        def act_dir(act, h, z):
            A, B, C, KI = dir_bufs(z)
            zb = ps[z][:, :]
            wait_product(act, "od_heads", 4 * h + z)
            if h >= 1:
                act.wait_ge(sem("increments"), 2 * (h - 1) + z + 1)
            act.activation(A, zb, ACT.Sigmoid)
            act.activation(B, zb, ACT.Sigmoid, scale=-1.0).then_inc(sem(f"z_kept{z}"), 1)
            act.wait_ge(sem(f"gate_made{z}"), h + 1)
            act.activation(A, A, ACT.Ln).then_inc(sem(f"log_made{z}"), 1)
            act.wait_ge(sem(f"summed{z}"), h + 1)
            act.activation(A, C, ACT.Exp)
            act.activation(KI, C[:, 0:S], ACT.Exp, scale=-1.0).then_inc(sem(f"exp_made{z}"), 1)
            act.wait_ge(sem(f"rest_made{z}"), h + 1)
            act.activation(C, C, ACT.Exp).then_inc(sem(f"decay_made{z}"), 1)

        def act_heads(act, own):
            first = BASE["od_heads"]
            for h in range(HG + 1):
                if h < HG:
                    act_part(act, first + 4 * h + HI)
                    act_dir(act, h, 0)
                    act_part(act, first + 4 * h + 1 + HI)
                    act_dir(act, h, 1)
                    act_part(act, first + 4 * h + 2 + HI)
                if h >= 1:
                    act_finish(act, h - 1)
                if h < HG:
                    act_part(act, first + 4 * h + 3 + HI)
                    wait_product(act, "od_heads", 4 * h + 3)
                    act.activation(qbuf, ps[2][:, 0:S], ACT.Copy).then_inc(sem("qg_kept"), 1)
                    if h >= 1:
                        act.wait_ge(sem("head_done"), h)
                    act.activation(gbuf, ps[2][:, S:N2], ACT.Silu).then_inc(sem("qg_kept"), 1)

        def dve_dir(dve, own, h, z):
            A, B, C, KI = dir_bufs(z)
            dve.wait_ge(sem(f"z_kept{z}"), h + 1)
            hc = slice(z * HG + h, z * HG + h + 1)
            own(dve.tensor_scalar(A, A, oml_c[:, hc], lbc[:, hc], ALU.mult, ALU.add), f"gate_made{z}")
            own(dve.tensor_scalar(B, B, oml_c[:, hc], None, ALU.mult))
            dve.wait_ge(sem(f"log_made{z}"), h + 1)
            a, c = (A, C) if z == 0 else (A[:, ::-1], C[:, ::-1])
            own(dve.tensor_tensor_scan(c, segmask, a, 0.0, ALU.mult, ALU.add), f"summed{z}")
            own(dve.tensor_copy(blast[z], chunk_end(C, z)))
            dve.wait_ge(sem(f"exp_made{z}"), h + 1)
            own(dve.tensor_copy(decay[z], chunk_end(A, z)))
            cc = C.rearrange("p (c n) -> p c n", n=CH)
            own(dve.tensor_tensor(cc, blast[z].unsqueeze(2).broadcast_to([P, NC2, CH]), cc, ALU.subtract), f"rest_made{z}")
            own(dve.tensor_tensor(KI, KI, B[:, 0:S], ALU.mult))
            dve.wait_ge(sem(f"decay_made{z}"), h + 1)
            own(dve.tensor_tensor(C, C, B, ALU.mult))

        def dve_states(dve, own, h, z):
            if h >= 1:
                dve.wait_ge(sem("o_done"), h)
            dve.wait_ge(sem("kd_turned"), 2 * h + z + 1)
            own(dve.tensor_copy(kdT[z], ps[3][:, :]), "kdt_kept")
            dve.wait_ge(sem("scored"), 2 * h + z + 1)
            for t in range(TT):
                ts = slice(t * P, (t + 1) * P)
                mm = dve.copy_predicated(scT[z][:, ts], cmask[z], ps[6][:, 2 * z * P + t * P:2 * z * P + (t + 1) * P])
            own(mm, "masked")
            dve.wait_ge(sem("increments"), 2 * h + z + 1)
            st = states[z]
            inc = lambda c: ps[4 + c % 2][:, (c // 2) * P:(c // 2 + 1) * P]
            first = list(order(z))
            s0 = st[:, first[0], :]
            own(dve.tensor_copy(s0, inc(4 + first[0])))
            for c in first[1:]:
                own(dve.scalar_tensor_tensor(s0, s0, decay[z][:, 4 + c:5 + c], inc(4 + c), ALU.mult, ALU.add))
            for n in range(3):
                c, nxt = first[n], first[n + 1]
                own(dve.scalar_tensor_tensor(st[:, nxt, :], st[:, c, :], decay[z][:, c:c + 1], inc(c), ALU.mult, ALU.add),
                    "states_done" if n == 2 else None)

        def act_finish(act, h):
            act.wait_ge(sem("o_done"), h + 1)
            act.activation(osq, ps[7][:, 0:S], ACT.Square).then_inc(sem("o_squared"), 1)
            act.wait_ge(sem("o_ms"), h + 1)
            act.activation(orms, orms, ACT.Sqrt).then_inc(sem("o_sqrt"), 1)

        def dve_finish(dve, own, h):
            dve.wait_ge(sem("o_summed"), h + 1)
            own(dve.tensor_scalar(orms, ps[7][:, S:N2], 1.0 / P, EPS, ALU.mult, ALU.add), "o_ms")
            dve.wait_ge(sem("o_sqrt"), h + 1)
            own(dve.reciprocal(orms, orms))
            own(dve.scalar_tensor_tensor(OT[:, h, :], ps[7][:, 0:S], pv("onorm", h, 1), orms, ALU.mult, ALU.mult))
            own(dve.tensor_tensor(OT[:, h, :], OT[:, h, :], gbuf, ALU.mult), "head_done")

        def dve_heads(dve, own):
            own(dve.memset(at(36864, 512), 0.0))
            dve.wait_ge(sem("masks_in"), 48)
            for h in range(HG + 1):
                for z in range(2):
                    if h >= 1:
                        dve_states(dve, own, h - 1, z)
                    if h < HG:
                        dve_dir(dve, own, h, z)
                if h == HG:
                    for i in range(HI):
                        dve_part(dve, BASE["od_out"] + i)
                if h >= 1:
                    dve_finish(dve, own, h - 1)
                if h < HG:
                    dve.wait_ge(sem("qg_kept"), 2 * h + 1)
                    for z in range(2):
                        own(dve.tensor_tensor(qd[z], dir_bufs(z)[0][:, 0:S], qbuf, ALU.mult), f"decayed{z}")

        def act_fin(act, own):
            X_ = operand(S)
            post_loads(act, "p1", 1)
            for g in range(4):
                act.activation(X_[0][:, 4 * g:4 * g + 4, :], OT[:, 4 * g:4 * g + 4, :], ACT.Copy).then_inc(sem("fin_hi"), 1)
            act_stream(act, "od_out")

        def dve_fin(dve, own):
            X_ = operand(S)
            for g in range(4):
                dve.wait_ge(sem("fin_hi"), g + 1)
                own(dve.tensor_tensor(X_[1][:, 4 * g:4 * g + 4, :], OT[:, 4 * g:4 * g + 4, :],
                                      X_[0][:, 4 * g:4 * g + 4, :].bitcast(F32), ALU.subtract), "fin_lo")
            for n in range(4):
                if n == 2:
                    post_gates(dve, own, "p1", 1)
                for c in range(4 * n, 4 * n + 4):
                    dve_part(dve, BASE["od_out"] + c + HI)
                wait_product(dve, "od_out", 4 * n + 3)
                for t in range(TT):
                    dve.tensor_copy(Y[:, t, n * 512:(n + 1) * 512], ps[2 * n + t][:, :]).then_inc(sem("y1_kept"), 1)

        def pe_fin(pe):
            pe_out(pe, "od_out", operand(S), TT, "y1_kept", lambda c: pe.wait_ge(sem("fin_lo"), c + 1))

        def for_half(step, half):
            pe_step, act_step, dve_step = step
            return (lambda pe: pe_step(pe, half), lambda act, own: act_step(act, own, half),
                    lambda dve, own: dve_step(dve, own, half))

        nothing = lambda *a: None
        gates, inner, outer = (pe_gates, act_gates, dve_gates), (pe_u, act_u, dve_u), (pe_v, act_v, dve_v)
        STAGES = [
            (pe_in, lambda a, o: (act_setup(a, o), act_in(a, o)), lambda v, o: (dve_setup(v, o), dve_in(v, o))),
            (pe_rec, act_rec, dve_rec),
            (pe_attn, act_attn, dve_attn),
            (lambda pe: pe_out(pe, "out", X, TT, "out1_kept"), lambda a, o: act_stream(a, "out"), dve_out1),
            (lambda pe: pe_norm(pe, "n2", res_tiles),
             lambda a, o: act_norm(a, o, "n2", [res[:, t, :] for t in range(TT)], S),
             lambda v, o: (dve_rms(v, o, "n2", TT), dve_diag(v, o, "n2", TT),
                           dve_norm(v, o, "n2", TT, S, lambda k, j: pv("ffn_g", k, 1), None))),
            (pe_query, act_query, dve_query),
            (pe_ada, act_top, lambda v, o: (dve_top(v, o), dve_ada(v, o))),
            *(for_half(step, half) for half in range(2) for step in (gates, inner, outer)),
            (lambda pe: pe_norm(pe, "n3", both_tiles), act_n3, dve_n3),
            (pe_even, act_even, dve_even),
            (pe_mix, act_mix, dve_mix),
            (pe_post, lambda a, o: act_post(a, o, "p0", 0, 4), lambda v, o: dve_post(v, o, "p0", 0, 4)),
            (pe_values, act_values, lambda v, o: (dve_n4(v, o), dve_values(v, o))),
            (pe_heads, act_heads, dve_heads),
            (pe_fin, act_fin, dve_fin),
            (nothing, lambda a, o: act_post(a, o, "p1", 1, 2), lambda v, o: dve_post(v, o, "p1", 1, 2)),
        ]

        block = ctx.enter_context(nc.Block())

        @block.sync
        def _(sp):
            sp.wait_ge(x_in, 16 * TT)
            for i in range(RAW):
                sp.dma_start(raw[i][:, :], d["stream"][i]).then_inc(landed[i], 16)
            turns = CHUNKS // RAW
            with sp.Fori(1, turns) as j:
                for r in range(RAW):
                    sp.wait_ge(used, j * RAW + (r + 1 - RAW))
                    sp.dma_start(raw[r][:, :], d["stream"][j * RAW + r]).then_inc(landed[r], 16)
            for i in range(turns * RAW, CHUNKS):
                sp.wait_ge(used, i + 1 - RAW)
                sp.dma_start(raw[i % RAW][:, :], d["stream"][i]).then_inc(landed[i % RAW], 16)

        @block.gpsimd
        def _(pool):
            def part(i, turn=None, step=0):
                v = rank_of(i) + 1
                pool.wait_ge(hi_by_act, v if turn is None else turn * step + v)
                pool.tensor_tensor(lo[i % RAW][:, :], raw[i % RAW][:, :], hi[i % HI][:, :].bitcast(F32),
                                   ALU.subtract).then_inc(split["pool"], 1)

            def split_run(run):
                first = BASE[run[0]]
                end = BASE[run[-1]] + COUNT[run[-1]]
                turns = (end - first) // RAW
                if turns > 0:
                    with pool.Fori(0, turns) as j:
                        for r in range(RAW):
                            part(first + r, j, RAW)
                for i in range(first + turns * RAW, end):
                    part(i)

            for run in RUNS[:2]:
                split_run(run)
            for half in range(2):
                pool_gates(pool, half)
            for run in RUNS[2:]:
                split_run(run)

        @block.tensor
        def _(pe):
            for stage in STAGES:
                stage[0](pe)
                rejoin(pe, "pe")

        @block.scalar
        def _(act):
            own = Own(act, "act_own", sem)
            for stage in STAGES:
                stage[1](act, own)
                rejoin(act, "act")

        @block.vector
        def _(dve):
            own = Own(dve, "dve_own", sem)
            for stage in STAGES:
                stage[2](dve, own)
                rejoin(dve, "dve")



def token_chunks(w):
    k, n = w.shape
    return w.reshape(k // 512, 4, P, n // 512, 512).transpose(3, 0, 2, 1, 4).reshape(-1, P, COLS)


def channel_chunks(w):
    k, n = w.shape
    return w.reshape(k // P, P, n // P, P).transpose(2, 1, 0, 3).reshape(-1, P, COLS)


def padded(a):
    out = np.zeros((a.shape[0], P, COLS), np.float32)
    out[:, :, :a.shape[2]] = a
    return out


def columns(v):
    return np.ascontiguousarray(v.reshape(-1, P).T)


def layout(i):
    w_in = i["w_in"][0]
    tok = w_in[:, :CQW].reshape(8, 2, P, CQW).transpose(0, 2, 1, 3).reshape(8, P, 2 * CQW)
    gates = np.concatenate([i["w_rgate"][0], i["w_igate"][0]]).transpose(1, 0, 2).reshape(1, P, COLS)
    ukv = i["w_ukv"][0].reshape(2, P, 2, 1024).transpose(2, 1, 0, 3).reshape(2, P, COLS)
    keys = np.stack([i["peer_keys_1"][0], i["peer_keys_2"][0]], 1).reshape(16, KEYS, P)
    keys = keys.transpose(2, 0, 1).reshape(1, P, COLS)
    parts = {
        "in_tok": padded(tok), "in_ch": channel_chunks(w_in[:, CQW:]), "gates": gates,
        "uq": token_chunks(i["w_uq"][0]), "ukv": ukv, "out": token_chunks(i["w_out"][0]),
        "wq": channel_chunks(i["peer_w_q"][0]), "keys": keys,
        "ev_a": ev_in_chunks(i["ev_w_in_2"][0])[:8], "ev_b": ev_in_chunks(i["ev_w_in_2"][0])[8:],
        "pool": i["ev_pool_w_2"][0].reshape(4, 2, P, 256).transpose(2, 0, 1, 3).reshape(1, P, COLS),
        "ev_out": token_chunks(i["ev_w_out_2"][0]),
        "od_v": token_chunks(i["od_w_in_2"][0][:, 4096:6144]),
        "od_heads": head_chunks(i["od_w_in_2"][0]),
        "od_out": token_chunks(i["od_w_out_2"][0]),
    }
    ada = [token_chunks(w).reshape(12, 4, P, COLS) for w in i["ada_w_2"]]
    at = 0
    for name, count, _ in SEGMENTS:
        if name.startswith("ada_"):
            parts[name] = np.concatenate([ada[layer][n] for layer, n in ADA[at:at + count // 4]])
            at += count // 4
    u, v = i["peer_u"][0], i["peer_v"][0]
    for half in range(2):
        rows = slice(half * HALF * P, (half + 1) * HALF * P)
        parts[f"u{half}"] = u[rows].reshape(HALF, P, KT, P).transpose(0, 3, 2, 1).reshape(HALF, P, COLS)
        parts[f"v{half}"] = v[rows].reshape(HALF, P, COLS)
    stream = np.empty((CHUNKS, P, COLS), np.float32)
    for name, count, _ in SEGMENTS:
        assert parts[name].shape[0] == count, name
        stream[BASE[name]:BASE[name] + count] = parts[name]
    p = {"mix_g": i["mix_norm_g"], "q_g": i["q_norm_g"], "kv_g": i["kv_norm_g"], "conv_w": i["conv_w"],
         "conv_b": i["conv_b"], "b_rg": i["b_rgate"], "b_ig": i["b_igate"], "lam": i["lru_lambda"],
         "attn_g": i["attn_out_norm_g"], "rec_g": i["rec_out_norm_g"], "ffn_g": i["ffn_norm_g"],
         "pre_g": i["pre_g_2"], "ada_b": i["ada_b_2"][:, :4096], "pool_scale": i["ev_pool_scale_2"],
         "conv2_w": i["ev_conv_w_2"], "conv2_b": i["ev_conv_b_2"], "onorm": i["od_onorm_g_2"],
         "lb": i["lb_logits_2"], "c": i["c_2"], "c_ctx": i["c_ctx_2"]}
    params = np.concatenate([columns(np.asarray(p[name])) for name, _ in PV_PARTS], 1)
    return {
        "stream": stream, "params": params, "consts": constants(), "x": i["x"][0], "ctx": i["ctx_2"][0],
        "positions": np.ascontiguousarray(i["positions"][0].reshape(TT, P).T),
        "q_head_g": i["q_head_norm_g"], "k_head_g": i["k_head_norm_g"],
        "post_g": i["post_g_2"], "ada_b_gate": i["ada_b_2"][:, 4096:], "tables": tables(),
    }


def ev_in_chunks(w):
    c = channel_chunks(w).reshape(6, 8, P, COLS)
    b = c[[2, 4, 3, 5]].transpose(1, 0, 2, 3).reshape(32, P, COLS)
    return np.concatenate([c[0], c[1], b])


def head_chunks(w):
    c = channel_chunks(w).reshape(5, HG, P, COLS)
    return c[[0, 1, 3, 4]].transpose(1, 0, 2, 3).reshape(4 * HG, P, COLS)


def constants():
    c = np.zeros((P, CNN), np.float32)

    def put(name, a):
        c[:, CN[name][0]:CN[name][1]] = a
    put("ident", np.eye(P))
    put("ones", 1.0)
    put("iota", np.arange(P)[None])
    put("iota16", np.arange(16)[None])
    put("causal", np.where(np.arange(P)[None] <= np.arange(P)[:, None], 0.0, -1e30))
    put("inv_freq", (10000.0 ** (-np.arange(32) / 32)).astype(np.float32)[None])
    put("sel_lat", np.arange(P)[:, None] == 0)
    put("sel_ctx", np.arange(P)[:, None] == 1)
    put("sel2", np.arange(P)[:, None] == np.arange(2)[None])
    return c


def tables():
    def count(n, w):
        t = np.arange(n)
        return np.minimum(t + w // 2 - 1, n - 1) - np.maximum(t - w // 2, 0) + 1.0
    parts = []
    for w in WINDOWS:
        parts.append((1.0 / np.outer(count(S // GRID_W, w), count(GRID_W, w))).ravel())
        parts.append(1.0 / count(S, w))
    parts.append((np.arange(2 * S) % CH != 0) * 1.0)
    rows = np.broadcast_to(np.concatenate(parts)[None], (P, 5 * 2 * S))
    s, c = np.arange(P)[:, None], np.arange(P)[None]
    same = s // CH == c // CH
    return np.concatenate([rows, same & (s <= c), same & (s >= c)], 1).astype(np.float32)


def kernel(**inputs):
    import concourse.bacc as bacc
    from concourse.bass_utils import run_bass_kernel_spmd

    arrays = layout({k: np.asarray(v) for k, v in inputs.items()})
    nc = bacc.Bacc("TRN2", target_bir_lowering=False, num_devices=1)
    d = {}
    for name, a in arrays.items():
        arrays[name] = a = np.ascontiguousarray(a)
        d[name] = nc.dram_tensor(name, a.shape, mybir.dt.from_np(a.dtype), kind="ExternalInput").ap()
    out = nc.dram_tensor("out", (S, D), F32, kind="ExternalOutput").ap()
    build(nc, d, out)
    r = run_bass_kernel_spmd(nc, [arrays], core_ids=[0])
    return r.results[0]["out"].reshape(1, S, D)
```
